# Optimizing a Trainium2 kernel written in Bass

```python
import functools
import jax, jax.numpy as jnp
from jax import lax
import numpy as np

D_MODEL = 2048
BATCH = 1
SEQ = 256
DEPTH = 2
DEC_BATCH = 8
DEC_SEQ = 1
PAST_LEN = 2048
PAGE_SIZE = 128

MIX_WIDTH = D_MODEL
N_MEM = 256
MEM_HEADS = 4
MEM_HEAD_DIM = 128
MEM_WIDTH = MEM_HEADS * MEM_HEAD_DIM
TOK_WIDTH = MIX_WIDTH - MEM_WIDTH
FOX_HEAD_DIM = 128
FOX_HEADS = TOK_WIDTH // FOX_HEAD_DIM
RWKV_HEAD_DIM = 64
RWKV_HEADS = TOK_WIDTH // RWKV_HEAD_DIM
DECAY_LORA = 96
ICLR_LORA = 96
SHIFT_DIM = 3 * TOK_WIDTH + DECAY_LORA + ICLR_LORA
FOX_IN = 3 * TOK_WIDTH + FOX_HEADS + MEM_WIDTH + MIX_WIDTH
RWKV_IN = SHIFT_DIM + MEM_WIDTH + MIX_WIDTH
FOX_SPLITS = (TOK_WIDTH, 2 * TOK_WIDTH, 3 * TOK_WIDTH, 3 * TOK_WIDTH + FOX_HEADS, 3 * TOK_WIDTH + FOX_HEADS + MEM_WIDTH)
RWKV_SPLITS = (SHIFT_DIM, SHIFT_DIM + MEM_WIDTH)
SHIFT_SPLITS = (TOK_WIDTH, 2 * TOK_WIDTH, 3 * TOK_WIDTH, 3 * TOK_WIDTH + DECAY_LORA)
N_FOX_LAYERS = (DEPTH + 1) // 2
N_RWKV_LAYERS = DEPTH // 2
Q_BLOCK = 128
RMS_EPS = 1e-6
GN_EPS = 64e-5
NEG_INF = -1e30
CACHE_FORGET_BIAS = 9.0

kernel_name = 'fox_rwkv7_memxattn_decode_step'

def rmsnorm(x, g):
    xf = x.astype(jnp.float32)
    y = xf * lax.rsqrt(jnp.mean(xf * xf, axis=-1, keepdims=True) + RMS_EPS)
    return (y * g.astype(jnp.float32)).astype(x.dtype)

def memory_kv(mem, g_mem, w_mem):
    b = mem.shape[0]
    k, v = jnp.split(rmsnorm(mem, g_mem) @ w_mem, 2, axis=-1)
    shape = (b, N_MEM, MEM_HEADS, MEM_HEAD_DIM)
    return k.reshape(shape), v.reshape(shape)

def memory_attend(q_mem, mem_k, mem_v):
    b, t, _ = q_mem.shape
    q = q_mem.reshape(b, t, MEM_HEADS, MEM_HEAD_DIM)
    s = jnp.einsum('bthd,bmhd->bhtm', q, mem_k).astype(jnp.float32) * (MEM_HEAD_DIM ** -0.5)
    p = jax.nn.softmax(s, axis=-1).astype(mem_v.dtype)
    return jnp.einsum('bhtm,bmhd->bthd', p, mem_v).reshape(b, t, MEM_WIDTH)

def gated_output(o_tok, o_mem, gate, w_o):
    o = jnp.concatenate([o_tok.astype(gate.dtype), o_mem.astype(gate.dtype)], axis=-1)
    return (o * jax.nn.silu(gate)) @ w_o

def suffix_logf(logf):
    return lax.cumsum(logf, axis=1, reverse=True) - logf

def fox_attend(q, k, v, d_q, d_k, q_pos, k_pos):
    s = jnp.einsum('bqhd,bkhd->bhqk', q, k).astype(jnp.float32) * (FOX_HEAD_DIM ** -0.5)
    s = s + jnp.transpose(d_k, (0, 2, 1))[:, :, None, :] - jnp.transpose(d_q, (0, 2, 1))[:, :, :, None]
    causal = k_pos[None, :] <= q_pos[:, None]
    s = jnp.where(causal[None, None], s, NEG_INF)
    p = jax.nn.softmax(s, axis=-1)
    return jnp.einsum('bhqk,bkhd->bqhd', p.astype(v.dtype), v)

def fox_prompt(q, k, v, logf):
    b, t = q.shape[:2]
    d = suffix_logf(logf)
    k_pos = jnp.arange(t)

    def one_block(blk):
        start = blk * Q_BLOCK
        qb = lax.dynamic_slice_in_dim(q, start, Q_BLOCK, axis=1)
        db = lax.dynamic_slice_in_dim(d, start, Q_BLOCK, axis=1)
        return fox_attend(qb, k, v, db, d, start + jnp.arange(Q_BLOCK), k_pos)

    o = lax.map(one_block, jnp.arange(t // Q_BLOCK))
    return jnp.moveaxis(o, 0, 1).reshape(b, t, TOK_WIDTH)

def fox_sample(q, k, v, logf, k_pool, v_pool, logf_pool, page_table):
    db, ds = q.shape[:2]
    k_past = k_pool[page_table].reshape(db, -1, FOX_HEADS, FOX_HEAD_DIM)
    v_past = v_pool[page_table].reshape(db, -1, FOX_HEADS, FOX_HEAD_DIM)
    f_past = logf_pool[page_table].reshape(db, -1, FOX_HEADS).astype(jnp.float32)
    past = k_past.shape[1]
    k_all = jnp.concatenate([k_past, k], axis=1)
    v_all = jnp.concatenate([v_past, v], axis=1)
    d = suffix_logf(jnp.concatenate([f_past, logf], axis=1))
    o = fox_attend(q, k_all, v_all, d[:, past:], d, past + jnp.arange(ds), jnp.arange(past + ds))
    return o.reshape(db, ds, TOK_WIDTH)

def fox_layer(x, g_pre, g_post, w_in, b_f, w_o, mem_k, mem_v, attend):
    b, t, _ = x.shape
    h = rmsnorm(x, g_pre)
    q, k, v, f, q_mem, gate = jnp.split(h @ w_in, FOX_SPLITS, axis=-1)
    hs = (b, t, FOX_HEADS, FOX_HEAD_DIM)
    q, k, v = q.reshape(hs), k.reshape(hs), v.reshape(hs)
    logf = jax.nn.log_sigmoid((f + b_f).astype(jnp.float32))
    o_tok = attend(q, k, v, logf)
    o_mem = memory_attend(q_mem, mem_k, mem_v)
    y = gated_output(o_tok, o_mem, gate, w_o)
    return x + rmsnorm(y, g_post), (k, v, logf)

def wkv_recurrence(r, decay, k, v, kk, a, wkv0):
    def step(S, inp):
        r_t, w_t, k_t, v_t, kk_t, a_t = inp
        sa = jnp.einsum('bhvk,bhk->bhv', S, -kk_t)
        S = S * w_t[:, :, None, :] + sa[..., None] * (kk_t * a_t)[:, :, None, :] + v_t[..., None] * k_t[:, :, None, :]
        return S, jnp.einsum('bhvk,bhk->bhv', S, r_t)

    xs = tuple(jnp.moveaxis(z, 1, 0) for z in (r, decay, k, v, kk, a))
    S, ys = lax.scan(step, wkv0, xs)
    return jnp.moveaxis(ys, 0, 1), S

def rwkv_layer(x, g_pre, g_post, w_in, mu, w0, w_w2, a0, w_a2, k_k, k_a, r_k, ln_w, ln_b,
               w_o, mem_k, mem_v, shift_prev, wkv0):
    f32 = jnp.float32
    b, t, _ = x.shape
    h = rmsnorm(x, g_pre)
    p_shift, q_mem, gate = jnp.split(h @ w_in, RWKV_SPLITS, axis=-1)
    prev = jnp.concatenate([shift_prev.astype(p_shift.dtype), p_shift[:, :-1]], axis=1)
    s = p_shift + (prev - p_shift) * mu
    r, k, v, wl, al = jnp.split(s, SHIFT_SPLITS, axis=-1)
    w = -jax.nn.softplus(-(w0 + jnp.tanh(wl) @ w_w2).astype(f32)) - 0.5
    decay = jnp.exp(-jnp.exp(w))
    a = jax.nn.sigmoid((a0 + al @ w_a2).astype(f32))
    kf = k.astype(f32)
    hs = (b, t, RWKV_HEADS, RWKV_HEAD_DIM)
    kk = (kf * k_k).reshape(hs)
    kk = kk / jnp.maximum(jnp.sqrt(jnp.sum(kk * kk, axis=-1, keepdims=True)), 1e-12)
    k_mod = (kf * (1.0 + (a - 1.0) * k_a)).reshape(hs)
    r_h = r.astype(f32).reshape(hs)
    v_h = v.astype(f32).reshape(hs)
    y, wkv = wkv_recurrence(r_h, decay.reshape(hs), k_mod, v_h, kk, a.reshape(hs), wkv0.astype(f32))
    mean = jnp.mean(y, axis=-1, keepdims=True)
    var = jnp.mean(jnp.square(y - mean), axis=-1, keepdims=True)
    yn = ((y - mean) * lax.rsqrt(var + GN_EPS)).reshape(b, t, TOK_WIDTH) * ln_w + ln_b
    bonus = jnp.sum(r_h * k_mod * r_k.astype(f32).reshape(RWKV_HEADS, RWKV_HEAD_DIM), axis=-1, keepdims=True) * v_h
    o_tok = yn + bonus.reshape(b, t, TOK_WIDTH)
    o_mem = memory_attend(q_mem, mem_k, mem_v)
    out = gated_output(o_tok, o_mem, gate, w_o)
    return x + rmsnorm(out, g_post), (wkv, p_shift[:, -1:])

def setup_inputs(seed: int = 0) -> dict:
    key = jax.random.key(seed)
    ks = jax.random.split(key, 32)
    f32 = jnp.float32

    def nrm(k, shape, scale=1.0):
        return jax.random.normal(k, shape, f32) * scale

    n_pages = PAST_LEN // PAGE_SIZE
    n_used = DEC_BATCH * n_pages
    n_pool = n_used + n_used // 4
    page_table = jax.random.permutation(ks[0], n_pool)[:n_used].reshape(DEC_BATCH, n_pages).astype(jnp.int32)
    return {
        'x_prompt': nrm(ks[1], (BATCH, SEQ, D_MODEL)),
        'x_sample': nrm(ks[2], (DEC_BATCH, DEC_SEQ, D_MODEL)),
        'cache_fox_k': nrm(ks[3], (N_FOX_LAYERS, n_pool, PAGE_SIZE, FOX_HEADS, FOX_HEAD_DIM)),
        'cache_fox_v': nrm(ks[4], (N_FOX_LAYERS, n_pool, PAGE_SIZE, FOX_HEADS, FOX_HEAD_DIM)),
        'cache_fox_logf': jax.nn.log_sigmoid(nrm(ks[5], (N_FOX_LAYERS, n_pool, PAGE_SIZE, FOX_HEADS)) + CACHE_FORGET_BIAS),
        'cache_mem_k': nrm(ks[6], (DEPTH, DEC_BATCH, N_MEM, MEM_HEADS, MEM_HEAD_DIM)),
        'cache_mem_v': nrm(ks[7], (DEPTH, DEC_BATCH, N_MEM, MEM_HEADS, MEM_HEAD_DIM)),
        'state_rwkv_wkv': nrm(ks[8], (N_RWKV_LAYERS, DEC_BATCH, RWKV_HEADS, RWKV_HEAD_DIM, RWKV_HEAD_DIM)),
        'state_rwkv_shift': nrm(ks[9], (N_RWKV_LAYERS, DEC_BATCH, 1, SHIFT_DIM)),
        'page_table': page_table,
        'mem_prompt': nrm(ks[10], (BATCH, N_MEM, D_MODEL)),
        'g_pre': 1.0 + nrm(ks[11], (DEPTH, D_MODEL), 0.05),
        'g_post': 1.0 + nrm(ks[12], (DEPTH, D_MODEL), 0.05),
        'g_mem': 1.0 + nrm(ks[13], (DEPTH, D_MODEL), 0.05),
        'w_mem': nrm(ks[14], (DEPTH, D_MODEL, 2 * MEM_WIDTH), D_MODEL ** -0.5),
        'w_o': nrm(ks[15], (DEPTH, MIX_WIDTH, D_MODEL), MIX_WIDTH ** -0.5),
        'fox_w_in': nrm(ks[16], (N_FOX_LAYERS, D_MODEL, FOX_IN), D_MODEL ** -0.5),
        'fox_b_f': jax.random.uniform(ks[17], (N_FOX_LAYERS, FOX_HEADS), f32, 1.0, 4.0),
        'rwkv_w_in': nrm(ks[18], (N_RWKV_LAYERS, D_MODEL, RWKV_IN), D_MODEL ** -0.5),
        'rwkv_mu': jax.random.uniform(ks[19], (N_RWKV_LAYERS, SHIFT_DIM), f32),
        'rwkv_w0': jax.random.uniform(ks[20], (N_RWKV_LAYERS, TOK_WIDTH), f32, -6.0, -1.0),
        'rwkv_w_w2': nrm(ks[21], (N_RWKV_LAYERS, DECAY_LORA, TOK_WIDTH), 0.5 * DECAY_LORA ** -0.5),
        'rwkv_a0': nrm(ks[22], (N_RWKV_LAYERS, TOK_WIDTH), 0.5),
        'rwkv_w_a2': nrm(ks[23], (N_RWKV_LAYERS, ICLR_LORA, TOK_WIDTH), 0.5 * ICLR_LORA ** -0.5),
        'rwkv_k_k': 0.85 + nrm(ks[24], (N_RWKV_LAYERS, TOK_WIDTH), 0.05),
        'rwkv_k_a': 1.0 + nrm(ks[25], (N_RWKV_LAYERS, TOK_WIDTH), 0.05),
        'rwkv_r_k': nrm(ks[26], (N_RWKV_LAYERS, TOK_WIDTH), 0.1),
        'rwkv_ln_w': 1.0 + nrm(ks[27], (N_RWKV_LAYERS, TOK_WIDTH), 0.05),
        'rwkv_ln_b': nrm(ks[28], (N_RWKV_LAYERS, TOK_WIDTH), 0.01),
    }

def reference(x_prompt, x_sample, cache_fox_k, cache_fox_v, cache_fox_logf, cache_mem_k, cache_mem_v,
              state_rwkv_wkv, state_rwkv_shift, page_table, mem_prompt,
              g_pre, g_post, g_mem, w_mem, w_o, fox_w_in, fox_b_f,
              rwkv_w_in, rwkv_mu, rwkv_w0, rwkv_w_w2, rwkv_a0, rwkv_w_a2,
              rwkv_k_k, rwkv_k_a, rwkv_r_k, rwkv_ln_w, rwkv_ln_b):
    xp, xs = x_prompt, x_sample
    b_prompt = x_prompt.shape[0]
    mem_k_new, mem_v_new = [], []
    fox_k_p, fox_v_p, fox_f_p, fox_k_s, fox_v_s, fox_f_s = [], [], [], [], [], []
    wkv_p, shift_p, wkv_s, shift_s = [], [], [], []
    for i in range(DEPTH):
        j = i // 2
        mk_p, mv_p = memory_kv(mem_prompt, g_mem[i], w_mem[i])
        mem_k_new.append(mk_p)
        mem_v_new.append(mv_p)
        if i % 2 == 0:
            attend_s = functools.partial(fox_sample, k_pool=cache_fox_k[j], v_pool=cache_fox_v[j],
                                         logf_pool=cache_fox_logf[j], page_table=page_table)
            xp, (k_p, v_p, f_p) = fox_layer(xp, g_pre[i], g_post[i], fox_w_in[j], fox_b_f[j], w_o[i],
                                            mk_p, mv_p, fox_prompt)
            xs, (k_s, v_s, f_s) = fox_layer(xs, g_pre[i], g_post[i], fox_w_in[j], fox_b_f[j], w_o[i],
                                            cache_mem_k[i], cache_mem_v[i], attend_s)
            fox_k_p.append(k_p)
            fox_v_p.append(v_p)
            fox_f_p.append(f_p)
            fox_k_s.append(k_s)
            fox_v_s.append(v_s)
            fox_f_s.append(f_s)
        else:
            shift0 = jnp.zeros((b_prompt, 1, SHIFT_DIM), xp.dtype)
            wkv0 = jnp.zeros((b_prompt, RWKV_HEADS, RWKV_HEAD_DIM, RWKV_HEAD_DIM), jnp.float32)
            xp, (st_p, sh_p) = rwkv_layer(xp, g_pre[i], g_post[i], rwkv_w_in[j], rwkv_mu[j], rwkv_w0[j],
                                          rwkv_w_w2[j], rwkv_a0[j], rwkv_w_a2[j], rwkv_k_k[j], rwkv_k_a[j],
                                          rwkv_r_k[j], rwkv_ln_w[j], rwkv_ln_b[j], w_o[i], mk_p, mv_p,
                                          shift0, wkv0)
            xs, (st_s, sh_s) = rwkv_layer(xs, g_pre[i], g_post[i], rwkv_w_in[j], rwkv_mu[j], rwkv_w0[j],
                                          rwkv_w_w2[j], rwkv_a0[j], rwkv_w_a2[j], rwkv_k_k[j], rwkv_k_a[j],
                                          rwkv_r_k[j], rwkv_ln_w[j], rwkv_ln_b[j], w_o[i],
                                          cache_mem_k[i], cache_mem_v[i], state_rwkv_shift[j], state_rwkv_wkv[j])
            wkv_p.append(st_p)
            shift_p.append(sh_p)
            wkv_s.append(st_s)
            shift_s.append(sh_s)
    return (xp, xs,
            jnp.stack(mem_k_new), jnp.stack(mem_v_new),
            jnp.stack(fox_k_p), jnp.stack(fox_v_p), jnp.stack(fox_f_p),
            jnp.stack(fox_k_s), jnp.stack(fox_v_s), jnp.stack(fox_f_s),
            jnp.stack(wkv_p), jnp.stack(shift_p),
            jnp.stack(wkv_s), jnp.stack(shift_s))


_drawn_inputs = setup_inputs


def setup_inputs(seed=0):
    import zlib

    import numpy as np

    out = dict(_drawn_inputs(seed))
    spreads = {}
    factors = {'cache_fox_logf': 27.644, 'rwkv_ln_b': 8.0}
    for name, (base, spread) in spreads.items():
        noise = np.random.default_rng([zlib.crc32(name.encode()), seed]).standard_normal(out[name].shape)
        drawn = base * np.exp(spread * noise) if base else spread * noise
        out[name] = __import__('jax').numpy.asarray(drawn.astype(out[name].dtype))
    for name, factor in factors.items():
        out[name] = (out[name] * factor).astype(out[name].dtype)
    return out
```

```python
from contextlib import ExitStack

import numpy as np

import concourse.bass as bass
from concourse import mybir

F32 = mybir.dt.float32
I32 = mybir.dt.int32
ALU = mybir.AluOpType
ACT = mybir.ActivationFunctionType
AX = mybir.AxisListType

P = 128
D = 2048
KT = D // P
NPR = 256
NS = 8
T = NPR + NS
NT = NPR // P
FH = 12
MH = 4
NMEM = 256
PAGES = 16
PAGE_W = FH * 128
RP = 12
LORA = 96
SHT = 38
U = 256
RW = 3 * P
OFF_W2 = KT * RW
OFF_A2 = OFF_W2 + P
OFF_V = OFF_A2 + P
OFF_SH = OFF_V + 10
RUNIT = OFF_SH + 3 * NS
KRING = 4
VRING = 4
SCALE = 128.0 ** -0.5
EXPM = float(np.exp(-0.5))
RMS_EPS = 1e-6
GN_EPS = 64e-5
LEVELS = 7
MU_R, MU_K, MU_V, W0, A0, K_K, K_A, R_K, LN_W, LN_B = range(10)

C_ID, C_ONE, C_BO, C_TRI, C_CAUS = 0, 128, 384, 512, 640
C_RM, C_LM, C_I64 = 768, 1280, 1280 + LEVELS * 128
C_N = C_I64 + 64


def shape_constants():
    s = np.arange(P)[:, None]
    t = np.arange(P)[None, :]
    c = np.zeros((P, C_N), np.float32)
    c[:, C_ID:C_ID + P] = s == t
    c[:, C_ONE:C_ONE + 256] = 1.0
    c[:, C_BO:C_BO + P] = s // 64 == t // 64
    c[:, C_TRI:C_TRI + P] = s > t
    c[:, C_CAUS:C_CAUS + P] = np.where(t <= s, 0.0, -1e30)
    for n in range(4):
        c[:, C_RM + n * P:C_RM + (n + 1) * P] = (s < t) if n % 2 == 0 else (s <= t)
    for n in range(LEVELS):
        m = 2 ** n
        c[:, C_LM + n * P:C_LM + (n + 1) * P] = (s // (2 * m) == t // (2 * m)) & (s % (2 * m) < m) & (t % (2 * m) >= m)
    c[:, C_I64:C_I64 + 64] = s % 64 == np.arange(64)[None, :]
    return c


M_MEM = (0, 80)
M_Q, M_QM0, M_KV, M_G0, M_WO0 = 8, 20, 24, 48, 64
M_LORA, M_QM1, M_RKV, M_G1, M_WO1 = 88, 90, 94, 130, 146
U_MEM = (0, 40)
U_Q, U_QM0, U_KV, U_G0, U_WO0 = 4, 10, 12, 24, 32
U_LORA, U_QM1, U_G1, U_WO1 = 44, 46, 48, 56


def trunk_step(nc, I, O):
    ctx = ExitStack()
    with ctx:
        def sb(name, shape, dt=F32):
            return ctx.enter_context(nc.sbuf_tensor(name, shape, dt))

        sems = {}

        def sem(name):
            if name not in sems:
                sems[name] = ctx.enter_context(nc.semaphore(name))
            return sems[name]

        xT = sb("xT", [P, KT, T])
        hT = sb("hT", [P, KT, T])
        oT = sb("oT", [P, KT, T])
        gT = sb("gT", [P, KT, T])
        wring = sb("wring", [P, 2, KT * U])
        kvr = sb("kvr", [P, 2 * RUNIT])
        cst = sb("cst", [P, C_N])
        kmT = sb("kmT", [P, MH, NMEM])
        vmr = sb("vmr", [P, NT, MH, P])
        gvec = sb("gvec", [P, 3, 2, KT])
        muL = sb("muL", [P, 2])
        shL = sb("shL", [P, 2, NS])
        shout = sb("shout", [P, SHT, 1 + NS])
        bf = sb("bf", [FH, 1])
        pts = sb("pts", [1, NS * PAGES], I32)
        arena = sb("arena", [P, 10120])

        class Region:
            def __init__(self, ap, size):
                self.ap, self.size, self.at = ap, size, 0

            def take(self, *shape, parts=P):
                n = int(np.prod(shape))
                a = self.ap[0:parts, self.at:self.at + n]
                self.at += n
                assert self.at <= self.size, (self.at, self.size)
                if len(shape) == 1:
                    return a
                names = "abc"[:len(shape)]
                return a.rearrange(f"p ({' '.join(names)}) -> p {' '.join(names)}",
                                   **{x: s for x, s in zip(names, shape)})

        psum = ctx.enter_context(nc.psum_tensor("psum", [P, 8, 512], F32))
        A, B, Wp, Y = (psum[:, n, :] for n in (2, 3, 4, 7))
        X = psum[:, 5:7, :]

        gflat = gT[:, :, :].rearrange("p k t -> p (k t)")
        kring = kvr[:, 0:KRING * PAGE_W].rearrange("p (r n) -> p r n", r=KRING)
        vring = kvr[:, KRING * PAGE_W:(KRING + VRING) * PAGE_W].rearrange("p (r n) -> p r n", r=VRING)
        runit = kvr[:, :].rearrange("p (r n) -> p r n", r=2)
        ident = cst[:, C_ID:C_ID + P]
        ones = cst[:, C_ONE:C_ONE + P]
        blockones = cst[:, C_BO:C_BO + P]

        r0 = Region(arena, 10120)
        qT = r0.take(KT, T)
        kvp = r0.take(4, T)
        lf = r0.take(NS * PAGES * FH)
        fpT = r0.take(T, parts=FH)
        frow = r0.take(NT, FH)
        dT = r0.take(NPR, parts=FH)
        ftmp = r0.take(T, parts=FH)
        kS = r0.take(FH, NS)
        vS = r0.take(FH, NS)
        selfS = r0.take(FH, NS)
        rs = r0.take(T)
        wfb = r0.take(KT, FH)
        base0 = r0.at
        qh = r0.take(2, T)
        dm = r0.take(2, NPR, parts=FH)
        vrow = r0.take(2, NT, P)
        nm = r0.take(2)
        rsum = r0.take(2)
        rinv = r0.take(2)
        rg = Region(gflat, KT * T)
        qd = rg.take(FH * P)
        qb = rg.take(FH * P)
        Pp = rg.take(2, NPR)
        PT = rg.take(2, NPR)
        r0.at = base0
        S = r0.take(PAGES * FH)
        Ps = r0.take(PAGES * FH)
        Fs = r0.take(PAGES * FH)
        mx = r0.take(FH)
        m12 = r0.take(1)
        dg = r0.take(FH)
        ld = r0.take(FH)
        mb = r0.take(FH)
        pse = r0.take(FH)
        ps = r0.take(FH)
        rden = r0.take(FH)
        osum = r0.take(FH)
        prod = r0.take(P)

        r1 = Region(arena, 10120)
        qT1 = r1.take(MH, T)
        wlT = r1.take(2, T)
        r1s = r1.at
        pb = r1.take(3, T + 1)
        sx = r1.take(3, T)
        df = r1.take(T)
        lw = r1.take(T)
        aa = r1.take(T)
        kkr = r1.take(T)
        kk = r1.take(T)
        km = r1.take(T)
        bb = r1.take(T)
        cc = r1.take(T)
        rn = r1.take(T)
        bonus = r1.take(T)
        yT = r1.take(T)
        E1 = r1.take(NPR)
        E2 = r1.take(NPR)
        KR = r1.take(NT, 2, P)
        bt = r1.take(NPR)
        kt = r1.take(NPR)
        s0 = r1.take(2, NS * 64)
        Cn = r1.take(P)
        SA = r1.take(P)
        ST = r1.take(64)
        S0p = r1.take(P)
        sc4 = r1.take(4)
        hs4 = r1.take(4)
        rg1 = Region(gflat, KT * T)
        rows = rg1.take(NT, 3, P)
        GM = rg1.take(4, 512)
        NM = rg1.take(4, P)
        Wsb = rg1.take(4 * P)
        TU = r1.take(4, 2 * P)
        Z = GM

        gpre = lambda l: gvec[:, 0, l, :]
        gpost = lambda l: gvec[:, 1, l, :]
        gmem = lambda l: gvec[:, 2, l, :]

        def val(i, per, k):
            return k if i is None else i * per + k

        ahead = ("stored_kv", "kv_free", "pair_done", "mix", "rw_out", "gm_out", "pair_stored_p", "y_out")

        def after(n):
            return n + 1

        class Chain:

            def __init__(self, eng, name):
                self.eng, self.s, self.n, self.i, self.per = eng, sem(name), 0, None, 0

            def do(self, ins):
                self.n += 1
                ins.then_inc(self.s, 1)
                self.eng.wait_ge(self.s, val(self.i, self.per, self.n))

            def enter(self, i, per):
                self.i, self.per, self.n0 = i, per, self.n

            def leave(self, count):
                assert self.n - self.n0 == self.per, f"{self.n - self.n0} steps an iteration, not {self.per}"
                self.n, self.i = self.n0 + count * self.per, None

        block = ctx.enter_context(nc.Block())

        @block.sync
        def _(sp):
            sp.dma_start(cst[:, :], I["consts"]).then_inc(sem("const_in"), 16)
            sp.dma_start(gflat[:, 0:KT * NMEM], I["memT"].rearrange("p k t -> p (k t)")).then_inc(sem("mem_in0"), 16)
            sp.dma_start(gvec[:, :, :, :].rearrange("p a l k -> p (a l k)"), I["gvec"]).then_inc(sem("vec_in"), 16)
            sp.dma_start(bf[:, :], I["bf"]).then_inc(sem("vec_in2"), 16)
            sp.dma_start(muL[:, :], I["muL"]).then_inc(sem("vec_in3"), 16)
            sp.dma_start(shL[:, :, :], I["shL"]).then_inc(sem("vec_in4"), 16)

            def unit(arr, index, slot):
                dst = wring[:, slot, :]
                if isinstance(index, int):
                    src = arr[index]
                else:
                    src = arr[bass.ds(index, 1)].rearrange("a p n -> (a p) n")
                sp.dma_start(dst[:, 0:src.shape[1]], src).then_inc(sem(f"w_full{slot}"), 16)

            def units(arr, count, m0):
                with sp.Fori(0, count // 2) as i:
                    for j in range(2):
                        index = sp.snap(i * 2 + j)
                        sp.wait_ge(sem("p_done"), val(i, 4, m0 + 2 * j - 2))
                        unit(arr, index, j)

            unit(I["wm0"], 0, 0)
            unit(I["wm0"], 1, 1)
            sp.dma_start(xT[:, :, :], I["xT"]).then_inc(sem("x_in"), 16)
            for n in range(2, 4):
                sp.wait_ge(sem("p_done"), 2 * n - 2)
                unit(I["wm0"], n, n % 2)
            units(I["wq"], 6, M_Q)
            units(I["wqm0"], 2, M_QM0)
            units(I["wkv"], 12, M_KV)
            units(I["wg0"], 8, M_G0)
            units(I["wo0"], 8, M_WO0)
            units(I["wm1"], 4, M_MEM[1])
            sp.wait_ge(sem("p_done"), M_MEM[1] + 8 - 2)
            unit(I["wl"], 0, 0)
            sp.wait_ge(sem("p_done"), M_MEM[1] + 8)
            unit(I["wl"], 1, 1)
            sp.wait_ge(sem("p_done"), M_LORA + 1)
            unit(I["wqm1"], 0, 0)
            sp.wait_ge(sem("p_done"), M_LORA + 2)
            unit(I["wqm1"], 1, 1)

            def rkv(index, j):
                if isinstance(index, int):
                    a, b = I["wrkv"][index], I["s0"][index]
                else:
                    a = I["wrkv"][bass.ds(index, 1)].rearrange("a p n -> (a p) n")
                    b = I["s0"][bass.ds(index, 1)].rearrange("a p n -> (a p) n")
                sp.dma_start(runit[:, j, :], a).then_inc(sem(f"r_full{j}"), 16)
                sp.dma_start(s0[:, j, :], b).then_inc(sem(f"s0_full{j}"), 16)

            sp.wait_ge(sem("ms_free"), 2 * NS + 2)
            for j in range(2):
                rkv(j, j)
            with sp.Fori(0, RP // 2 - 1) as i:
                for j in range(2):
                    sp.wait_ge(sem("pair_done"), after(val(i, 2, j + 1)))
                    rkv(i * 2 + (2 + j), j)
            units(I["wg1"], 8, M_G1)
            units(I["wo1"], 8, M_WO1)

        @block.gpsimd
        def _(pool):
            pool.dma_start(pts[:, :], I["pt"].rearrange("(a b) -> a b", a=1)).then_inc(sem("pt_in"), 16)
            pool.wait_ge(sem("pt_in"), 16)
            npool = I["ck"].shape[0]

            def page_id(s, g):
                return pool.value_load(pts[0:1, bass.ds(s * PAGES + g, 1)], min_val=0, max_val=npool - 1)

            def k_page(s, g, nth):
                if nth is not None:
                    pool.wait_ge(sem("k_used"), nth)
                pid = page_id(s, g)
                pool.dma_start(kring[:, g % KRING, :],
                               I["ck"][bass.ds(pid, 1)].rearrange("a p n -> (a p) n")).then_inc(sem(f"k_full{g % KRING}"), 16)
                pool.dma_start(lf[:, bass.ds((s * PAGES + g) * FH, FH)],
                               I["cf"][bass.ds(pid, 1)].rearrange("a p n -> (a p) n")).then_inc(sem(f"k_full{g % KRING}"), 16)

            def v_page(s, g, nth):
                if nth is not None:
                    pool.wait_ge(sem("v_used"), nth)
                pid = page_id(s, g)
                pool.dma_start(vring[:, g % VRING, :],
                               I["cv"][bass.ds(pid, 1)].rearrange("a p n -> (a p) n")).then_inc(sem(f"v_full{g % VRING}"), 16)

            for g in range(PAGES):
                k_page(0, g, g - KRING + 1 if g >= KRING else None)
            for g in range(PAGES):
                v_page(0, g, g - VRING + 1 if g >= VRING else None)
                k_page(1, g, PAGES + g - KRING + 1)
            with pool.Fori(1, NS - 1) as s:
                for g in range(PAGES):
                    v_page(s, g, s * PAGES + (g - VRING + 1))
                    k_page(s + 1, g, s * PAGES + (PAGES + g - KRING + 1))
            for g in range(PAGES):
                v_page(NS - 1, g, (NS - 1) * PAGES + g - VRING + 1)

            pool.wait_ge(sem("k_used"), NS * PAGES)
            pool.wait_ge(sem("v_used"), NS * PAGES)
            for layer in range(2):
                if layer == 1:
                    pool.wait_ge(sem("p_done"), M_WO0 + 16)
                    pool.dma_start(gflat[:, 0:KT * NMEM], I["memT"].rearrange("p k t -> p (k t)")).then_inc(sem("mem_in1"), 16)
                with pool.Fori(0, NS // 2) as i:
                    for j in range(2):
                        row = i * 2 + (layer * NS + j)
                        pool.wait_ge(sem("ms_free"), val(i, 2, layer * NS + j + 1))
                        for ring, name, full in ((kring, "cmk", "mk_full"), (vring, "cmv", "mv_full")):
                            pool.dma_start(ring[:, j, 0:1024].rearrange("p (t n) -> p t n", t=2),
                                           I[name][bass.ds(row, 1)].rearrange("a (t p) n -> p (a t) n", p=P))\
                                .then_inc(sem(f"{full}{j}"), 16)

        @block.tensor
        def _(pe):
            mm = nc.tensor.matmul

            def project(i, base_u, m0, rhs, n, width=P, tiles=2, srcs=None):
                for j in range(2):
                    pe.wait_ge(sem(f"w_full{j}"), val(i, 16, 16 * (base_u // 2 + 1)))
                    w = wring[:, j, 0:KT * tiles * width].rearrange("p (k n) -> p k n", k=KT)
                    for t in range(tiles):
                        m = m0 + j * tiles + t
                        pe.wait_ge(sem("p_free"), val(i, 2 * tiles, m + 1))
                        for k in range(KT):
                            last = mm(psum[0:width, m % 2, 0:n], w[:, k, t * width:(t + 1) * width], rhs[:, k, 0:n],
                                      start=(k == 0), stop=(k == KT - 1))
                        last.then_inc(sem("p_done"), 1)

            def sum_squares(o, buf, n):
                for k in range(KT):
                    if k % 4 == 0:
                        pe.wait_ge(sem("n_sq"), 4 * o + k // 4 + 1)
                    last = mm(A[:, 0:n], ones, buf[:, k, 0:n], start=(k == 0), stop=(k == KT - 1))
                last.then_inc(sem("n_ss"), 1)

            def memory(layer):
                o = (0, 3)[layer]
                sum_squares(o, oT, NMEM)
                pe.wait_ge(sem("n_out"), o + 1)
                project(None, U_MEM[layer], M_MEM[layer], oT, NMEM)
                project(None, U_MEM[layer] + 2, M_MEM[layer] + 4, oT, NMEM)
                for h in range(MH):
                    pe.wait_ge(sem("mv_t"), layer * MH + h + 1)
                    pe.wait_ge(sem("mr_out"), layer * MH + h)
                    for t in range(NT):
                        last = nc.tensor.transpose(B[:, t * P:(t + 1) * P], kvp[:, h, t * P:(t + 1) * P], ident)
                    last.then_inc(sem("mr_t"), 1)

            def attend_prompt(h, o, keys, queries, values, causal):
                pe.wait_ge(sem("at_e"), o)
                for t in range(NT):
                    if not causal:
                        last = mm(X[:, t, 0:NMEM], queries[:, t * P:(t + 1) * P], keys, start=True, stop=True)
                        continue
                    for b in range(t + 1):
                        ks = slice(b * P, (b + 1) * P)
                        mm(X[:, t, ks], queries[:, t * P:(t + 1) * P], keys[:, ks], start=True, stop=False)
                        mm(X[:, t, ks], cst[0:FH, C_ONE:C_ONE + P], dm[:, 0, ks], start=False, stop=False)
                        last = mm(X[:, t, ks], dm[:, 1, t * P:(t + 1) * P], cst[0:FH, C_ONE:C_ONE + P], start=False, stop=b < t)
                    last = mm(X[:, t, t * P:(t + 1) * P], ident, cst[:, C_CAUS:C_CAUS + P], start=False, stop=True)
                last.then_inc(sem("at_s"), 1)
                pe.wait_ge(sem("at_p"), o + 1)
                pe.wait_ge(sem("at_pt"), o)
                for t in range(NT):
                    for kt_ in range(NT):
                        if causal and kt_ > t:
                            continue
                        last = nc.tensor.transpose(B[:, kt_ * NPR + t * P:kt_ * NPR + (t + 1) * P],
                                                   Pp[:, t, kt_ * P:(kt_ + 1) * P], ident)
                last.then_inc(sem("at_t"), 1)
                pe.wait_ge(sem("at_pt"), o + 1)
                pe.wait_ge(sem("at_o"), o)
                if causal:
                    mm(Y[:, 0:P], values[:, 0, :], PT[:, 0, 0:P], start=True, stop=True)
                q0 = P if causal else 0
                mm(Y[:, q0:NPR], values[:, 0, :], PT[:, 0, q0:NPR], start=True, stop=False)
                mm(Y[:, q0:NPR], values[:, 1, :], PT[:, 1, q0:NPR], start=False, stop=True).then_inc(sem("at_y"), 1)

            def spread_queries(x, nh, i, per, o):
                pe.wait_ge(sem(x + "_qd"), val(i, per, o + 1))
                for c in range(nh // 4):
                    last = mm((Wp, X[:, 0, :], X[:, 1, :])[c], ones, qd[:, c * 512:(c + 1) * 512], start=True, stop=True)
                last.then_inc(sem(x + "_qb"), 1)

            def softmax_sample(s, x, nh, fox, i, per, o):
                if fox:
                    pe.wait_ge(sem(x + "_ld"), val(i, per, o + 1))
                    n = PAGES * FH
                    mm(A[:, 0:n], cst[:, C_TRI:C_TRI + P], lf[:, bass.ds(s * n, n)], start=True, stop=False)
                    mm(A[:, 0:n], ones, Fs, start=False, stop=False)
                    mm(A[:, 0:n].rearrange("p (g h) -> p g h", h=FH), cst[0:FH, C_ONE:C_ONE + P],
                       ld[0:FH, :].unsqueeze(1).to_broadcast([FH, PAGES, FH]), start=False, stop=True).then_inc(sem(x + "_b"), 1)
                pe.wait_ge(sem(x + "_mx"), val(i, per, o + 1))
                nc.tensor.transpose(B[0:nh, 0:P], mx[:, 0:nh], ident).then_inc(sem(x + "_mt"), 1)
                pe.wait_ge(sem(x + "_dg"), val(i, per, o + 1))
                mm(A[:, 256:256 + nh], cst[0:nh, C_ONE:C_ONE + P], dg[0:nh, 0:nh], start=True, stop=True).then_inc(sem(x + "_mb"), 1)
                pe.wait_ge(sem(x + "_ps"), val(i, per, o + 1))
                mm(A[:, 256:256 + nh], ones, ps[:, 0:nh], start=True, stop=True).then_inc(sem(x + "_den"), 1)

            def weigh_values(nh, ng, fox, full, slots):
                for g in range(ng):
                    full(g)
                    for h in range(nh):
                        last = mm(Y[:, h:h + 1], slots(g, h), Ps[:, g * nh + h:g * nh + h + 1],
                                  start=(g == 0 and h == 0), stop=(g == ng - 1), skip_group_check=True)
                    if fox:
                        last.then_inc(sem("v_used"), 1)
                if not fox:
                    last.then_inc(sem("ms_pv"), 1)

            def memory_samples(layer):
                with pe.Fori(0, NS // 2) as i:
                    for j in range(2):
                        spread_queries("ms", MH, i, 2, layer * NS + j)
                        softmax_sample(None, "ms", MH, False, i, 2, layer * NS + j)
                        weigh_values(MH, 2, False,
                                     lambda g: pe.wait_ge(sem(f"mv_full{j}"), val(i, 16, 16 * (layer * NS // 2 + 1))),
                                     lambda g, h: vring[:, j, g * 512 + h * P:g * 512 + (h + 1) * P])

            pe.wait_ge(sem("const_in"), 16)
            memory(0)
            sum_squares(1, hT, T)
            pe.wait_ge(sem("n_out"), 2)
            with pe.Fori(0, 3) as i:
                project(i, U_Q, M_Q, hT, T)
            project(None, U_QM0, M_QM0, hT, T)
            pe.wait_ge(sem("wf_in"), 16)
            for k in range(KT):
                last = mm(A[0:FH, 0:T], wfb[:, k, :], hT[:, k, :], start=(k == 0), stop=(k == KT - 1))
            last.then_inc(sem("f_y"), 1)
            pe.wait_ge(sem("f_out"), 1)
            for t in range(NT):
                last = nc.tensor.transpose(B[:, t * FH:(t + 1) * FH], fpT[:, t * P:(t + 1) * P], ident[0:FH, 0:FH])
            last.then_inc(sem("f_t"), 1)
            pe.wait_ge(sem("f_row"), 1)
            mm(A[0:FH, 0:P], frow[:, 0, :], cst[:, C_TRI:C_TRI + P], start=True, stop=False)
            mm(A[0:FH, 0:P], frow[:, 1, :], ones, start=False, stop=True)
            mm(A[0:FH, P:2 * P], frow[:, 1, :], cst[:, C_TRI:C_TRI + P], start=True, stop=True).then_inc(sem("d_y"), 1)
            for h in range(MH):
                pe.wait_ge(sem("at_in"), h + 1)
                attend_prompt(h, h, kmT[:, h, :], qh[:, 0, :], vmr[:, :, h, :], False)
            with pe.Fori(0, FH // 2) as i:
                project(i, U_KV, M_KV, hT, T)
                pe.wait_ge(sem("kv_out"), val(i, 1, 1))
                pe.wait_ge(sem("at_pt"), val(i, 2, MH))
                for j in range(2):
                    for t in range(NT):
                        last = nc.tensor.transpose(B[:, (j * NT + t) * P:(j * NT + t + 1) * P],
                                                   kvp[:, 2 + j, t * P:(t + 1) * P], ident)
                last.then_inc(sem("vr_t"), 1)
                pe.wait_ge(sem("vr_out"), val(i, 1, 1))
                for j in range(2):
                    pe.wait_ge(sem("at_in"), val(i, 2, MH + j + 1))
                    o = i * 2 + (MH + j)
                    attend_prompt(None, o, kvp[:, j, 0:NPR], qh[:, j, 0:NPR], vrow[:, j, :, :], True)
            pe.wait_ge(sem("self_p"), 1)
            mm(A[:, 0:FH * NS], ones, prod[:, 0:FH * NS], start=True, stop=True).then_inc(sem("self_y"), 1)
            pe.wait_ge(sem("self_out"), 1)
            def page_values(s):
                weigh_values(FH, PAGES, True,
                             lambda g: pe.wait_ge(sem(f"v_full{g % VRING}"), s * (16 * PAGES // VRING) + 16 * (g // VRING + 1)),
                             lambda g, h: vring[:, g % VRING, h * P:(h + 1) * P])

            spread_queries("fs", FH, None, 1, 0)
            softmax_sample(0, "fs", FH, True, None, 1, 0)
            with pe.Fori(1, NS) as s:
                spread_queries("fs", FH, s, 1, 0)
                page_values(s - 1)
                softmax_sample(s, "fs", FH, True, s, 1, 0)
            page_values(NS - 1)
            memory_samples(0)
            with pe.Fori(0, 4) as i:
                project(i, U_G0, M_G0, hT, T)
            pe.wait_ge(sem("u_out"), 1)
            with pe.Fori(0, 4) as i:
                project(i, U_WO0, M_WO0, gT, T)
            sum_squares(2, hT, T)
            memory(1)
            sum_squares(4, hT, T)
            pe.wait_ge(sem("n_out"), 5)
            project(None, U_LORA, M_LORA, hT, T, width=LORA, tiles=1)
            project(None, U_QM1, M_QM1, hT, T)
            for h in range(MH):
                o = MH + FH + h
                pe.wait_ge(sem("at_in"), o + 1)
                attend_prompt(h, o, kmT[:, h, :], qh[:, 0, :], vmr[:, :, h, :], False)
            memory_samples(1)

            with pe.Fori(0, RP // 2) as i:
                for j in range(2):
                    o = i * 2 + j
                    w = runit[:, j, 0:OFF_W2].rearrange("p (k n) -> p k n", k=KT)
                    pe.wait_ge(sem(f"r_full{j}"), val(i, 16, 16))
                    for t in range(3):
                        m = M_RKV + 3 * j + t
                        pe.wait_ge(sem("p_free"), val(i, 6, m + 1))
                        for k in range(KT):
                            last = mm(psum[:, m % 2, 0:T], w[:, k, t * P:(t + 1) * P], hT[:, k, :],
                                      start=(k == 0), stop=(k == KT - 1))
                        last.then_inc(sem("p_done"), 1)
                    pe.wait_ge(sem("pair_done"), after(o))
                    mm(A[:, 0:T], runit[0:LORA, j, OFF_W2:OFF_W2 + P], wlT[0:LORA, 0, :], start=True, stop=True)
                    mm(Wp[:, 0:T], runit[0:LORA, j, OFF_A2:OFF_A2 + P], wlT[0:LORA, 1, :], start=True, stop=True)\
                        .then_inc(sem("wa_y"), 1)
                    pe.wait_ge(sem("wa_out"), o + 1)
                    pe.wait_ge(sem("kk_sq"), o + 1)
                    mm(A[:, 0:T], blockones, df, start=True, stop=True).then_inc(sem("kk_ss"), 1)
                    pe.wait_ge(sem("rk_p"), o + 1)
                    mm(Wp[:, 0:T], blockones, rn, start=True, stop=True).then_inc(sem("rk_y"), 1)
                    pe.wait_ge(sem("tl_in"), o + 1)
                    for c in range(NT):
                        pe.wait_ge(sem("rw_out"), after(o * 2 + c))
                        for n, src in enumerate((bt, kt, sx[:, 2, 0:NPR])):
                            last = nc.tensor.transpose(B[:, n * P:(n + 1) * P], src[:, c * P:(c + 1) * P], ident)
                        last.then_inc(sem("rw_t"), 1)
                    for q in range(4):
                        c, h = q // 2, q % 2
                        hp = slice(64 * h, 64 * h + 64)
                        pe.wait_ge(sem("gm_out"), after((o * 4 + (q - 1)) if q else o * 4))
                        mm(X[:, q % 2, 0:256], bt[hp, c * P:(c + 1) * P], KR[hp, c, :, :].rearrange("p a t -> p (a t)"),
                           start=True, stop=True)
                        mm(X[:, q % 2, 256:512], kt[hp, c * P:(c + 1) * P], KR[hp, c, :, :].rearrange("p a t -> p (a t)"),
                           start=True, stop=True).then_inc(sem("gm_y"), 1)
                    pe.wait_ge(sem("nm_out"), o * LEVELS + 1)
                    for q in range(4):
                        last = nc.tensor.transpose(Wp[:, q * P:(q + 1) * P], NM[:, q, :], ident)
                    last.then_inc(sem("lv_w"), 1)
                    for n in range(1, LEVELS):
                        pe.wait_ge(sem("nm_out"), o * LEVELS + (n + 1))
                        pe.wait_ge(sem("tu_out"), o * LEVELS + n)
                        for q in range(4):
                            last = mm(Wp[:, q * P:(q + 1) * P], NM[:, q, :], TU[:, q, 0:P], start=True, stop=True)
                        last.then_inc(sem("lv_w"), 1)
                        pe.wait_ge(sem("ws_out"), o * (LEVELS - 1) + n)
                        for q in range(4):
                            last = mm(X[:, q // 2, (q % 2) * 256:(q % 2) * 256 + P], TU[:, q, P:2 * P], Wsb[:, q * P:(q + 1) * P],
                                      start=True, stop=True)
                            last = mm(X[:, q // 2, (q % 2) * 256 + P:(q % 2) * 256 + 2 * P], Wsb[:, q * P:(q + 1) * P], TU[:, q, P:2 * P],
                                      start=True, stop=True)
                        last.then_inc(sem("lv_d"), 1)
                    pe.wait_ge(sem("tu_out"), o * LEVELS + LEVELS)
                    for c in range(NT):
                        if c:
                            pe.wait_ge(sem("st_in"), o + 1)
                        if c:
                            mm(Wp[:, 0:P], KR[:, c, 0, :], S0p, start=True, stop=False)
                        for h in range(2):
                            hp, q = slice(64 * h, 64 * h + 64), 2 * c + h
                            last = mm(Wp[:, hp], GM[:, q, 256:384], rows[:, c, 2, hp], start=c == 0, stop=c == 0 or h == 1)
                        last.then_inc(sem("c_y"), 1)
                        pe.wait_ge(sem("c_out"), o * 2 + c + 1)
                        for h in range(2):
                            hp, q = slice(64 * h, 64 * h + 64), 2 * c + h
                            last = mm(Wp[:, 128 + 64 * h:192 + 64 * h], TU[:, q, P:2 * P], Cn[:, hp], start=True, stop=True)
                        last.then_inc(sem("sa_y"), 1)
                        pe.wait_ge(sem("sa_out"), o * 2 + c + 1)
                        pe.wait_ge(sem("y_out"), after(o * 2 + c))
                        for h in range(2):
                            hp, q = slice(64 * h, 64 * h + 64), 2 * c + h
                            mm(Y[hp, 0:P], SA[:, hp], GM[:, q, 128:256], start=True, stop=False)
                            last = mm(Y[hp, 0:P], rows[:, c, 2, hp], GM[:, q, 384:512], start=False, stop=c == 0)
                            if c:
                                last = mm(Y[hp, 0:P], S0p[:, hp], KR[:, c, 1, :], start=False, stop=True)
                        for h in range(2):
                            hp = slice(64 * h, 64 * h + 64)
                            mm(Y[hp, 128:192], rows[:, c, 0, hp], SA[:, hp], start=True, stop=False)
                            last = mm(Y[hp, 128:192], rows[:, c, 1, hp], rows[:, c, 2, hp], start=False, stop=True)
                        last.then_inc(sem("y_y"), 1)
                    for n in range(3):
                        pe.wait_ge(sem("z_in"), o * 3 + (n + 1))
                        mm((X[:, 0, :], X[:, 1, :], Wp)[n], blockones, Z[:, n, :], start=True, stop=True).then_inc(sem("z_y"), 1)
                    pe.wait_ge(sem("gn_in"), o * 2 + 1)
                    mm(A[:, 0:T], blockones, yT, start=True, stop=True).then_inc(sem("gn_y"), 1)
                    pe.wait_ge(sem("gn_in"), o * 2 + 2)
                    mm(A[:, 0:T], blockones, df, start=True, stop=True).then_inc(sem("gn_y"), 1)
            with pe.Fori(0, 4) as i:
                project(i, U_G1, M_G1, hT, T)
            pe.wait_ge(sem("u_out"), 2)
            with pe.Fori(0, 4) as i:
                project(i, U_WO1, M_WO1, gT, T)
            sum_squares(5, hT, T)

        @block.scalar
        def _(act):
            ac = nc.scalar.activation
            ch = Chain(act, "act_step")
            act.dma_start(wfb, I["wf"]).then_inc(sem("wf_in"), 16)
            act.sem_inc(sem("p_free"), 2)

            def tile_out(i, per, m, dst, n, func=ACT.Copy, scale=1.0, width=P, then=None):
                act.wait_ge(sem("p_done"), val(i, per, m + 1))
                ac(dst, psum[0:width, m % 2, 0:n], func, scale=scale).then_inc(sem("p_free"), 1)

            def dyn(buf, i, k):
                return buf[:, bass.ds(i + k, 1), :].rearrange("p a t -> p (a t)")

            def root(o, buf):
                act.wait_ge(sem("n_ms"), o + 1)
                ac(buf, buf, ACT.Sqrt).then_inc(sem("n_rt"), 1)

            def memory(layer):
                root((0, 3)[layer], rs[:, 0:NMEM])
                for m in range(8):
                    dst = kmT[:, m, :] if m < 4 else kvp[:, m - 4, 0:NMEM]
                    act.wait_ge(sem("p_done"), M_MEM[layer] + m + 1)
                    if m >= 4:
                        ac(dst, psum[:, m % 2, 0:NMEM], ACT.Copy).then_inc(sem("mv_t"), 1)
                        act.wait_ge(sem("mv_t"), layer * MH + m - 3)
                        act.sem_inc(sem("p_free"), 1)
                    else:
                        ac(dst, psum[:, m % 2, 0:NMEM], ACT.Copy).then_inc(sem("p_free"), 1)
                act.wait_ge(sem("p_free"), M_MEM[layer] + 8 + 2)
                act.dma_start(O["mk"][layer], kmT[:, :, :].rearrange("p h t -> p (h t)")).then_inc(sem("stored_mem"), 16)
                act.dma_start(O["mv"][layer].rearrange("p (h t) -> p h t", h=MH), kvp[:, :, 0:NMEM]).then_inc(sem("stored_mem"), 16)
                for h in range(MH):
                    act.wait_ge(sem("mr_t"), layer * MH + h + 1)
                    ac(vmr[:, :, h, :], B[:, 0:NPR].rearrange("p (t n) -> p t n", t=NT), ACT.Copy).then_inc(sem("mr_out"), 1)
                act.wait_ge(sem("stored_mem"), 32 * (layer + 1))

            def attend_prompt(o, causal, dst):
                act.wait_ge(sem("at_m"), o + 1)
                for t in range(NT):
                    nk = P * (t + 1) if causal else NMEM
                    last = ac(Pp[:, t, 0:nk], X[:, t, 0:nk], ACT.Exp, bias=nm[:, t:t + 1], accum_out=rsum[:, t:t + 1])
                last.then_inc(sem("at_e"), 1)
                act.wait_ge(sem("at_t"), o + 1)
                act.wait_ge(sem("at_y"), o)
                if causal:
                    ac(PT[:, 0, :], B[:, 0:NPR], ACT.Copy)
                    ac(PT[:, 1, P:NPR], B[:, NPR + P:2 * NPR], ACT.Copy).then_inc(sem("at_pt"), 1)
                else:
                    ac(PT[:, :, :].rearrange("p a t -> p (a t)"), B[:, :], ACT.Copy).then_inc(sem("at_pt"), 1)
                act.wait_ge(sem("at_y"), o + 1)
                ac(dst, Y[:, 0:NPR], ACT.Copy).then_inc(sem("at_o"), 1)

            def attend_sample(x, nh, ng, i, per, o):
                act.wait_ge(sem(x + "_qb"), val(i, per, o + 1))
                if x == "ms":
                    act.wait_ge(sem("ms_free"), val(i, per, o + 2))
                else:
                    act.wait_ge(sem("k_used"), val(i, PAGES, PAGES * o))
                for c in range(nh // 4):
                    last = ac(qb[:, c * 512:(c + 1) * 512], (Wp, X[:, 0, :], X[:, 1, :])[c], ACT.Copy)
                last.then_inc(sem(x + "_qbs"), 1)
                act.wait_ge(sem(x + "_sub"), val(i, per, o + 1))
                if x == "fs":
                    ac(pse, pse, ACT.Exp)
                ac(Ps[:, 0:nh * ng], S[:, 0:nh * ng], ACT.Exp).then_inc(sem(x + "_e"), 1)

            def memory_samples(layer):
                with act.Fori(0, NS // 2) as i:
                    for j in range(2):
                        attend_sample("ms", MH, 2, i, 2, layer * NS + j)

            memory(0)
            root(1, rs)
            with act.Fori(0, 3) as i:
                for t in range(4):
                    tile_out(i, 4, M_Q + t, dyn(qT, i * 4, t), T, scale=SCALE)
            for t in range(4):
                tile_out(None, 4, M_QM0 + t, qT[:, FH + t, :], T, scale=SCALE)
            act.wait_ge(sem("f_abs"), 1)
            ch.do(ac(ftmp, ftmp, ACT.Exp, scale=-1.0))
            ac(ftmp, ftmp, ACT.Ln, bias=1.0).then_inc(sem("f_ln"), 1)
            act.wait_ge(sem("f_out"), 1)
            act.dma_start(O["lf"], fpT).then_inc(sem("stored_lf"), 16)
            act.wait_ge(sem("f_t"), 1)
            ac(frow.rearrange("p t h -> p (t h)"), B[:, 0:NT * FH], ACT.Copy).then_inc(sem("f_row"), 1)
            act.wait_ge(sem("d_y"), 1)
            ac(dT, A[0:FH, 0:NPR], ACT.Copy).then_inc(sem("d_out"), 1)
            for h in range(MH):
                attend_prompt(h, False, oT[:, FH + h, 0:NPR])
            with act.Fori(0, FH // 2) as i:
                act.wait_ge(sem("stored_kv"), after(val(i, 32, 0)))
                act.wait_ge(sem("kv_free"), after(val(i, 1, 0)))
                for t in range(4):
                    act.wait_ge(sem("p_done"), val(i, 4, M_KV + t + 1))
                    ac(kvp[:, t, :], psum[:, t % 2, 0:T], ACT.Copy)
                    ac((kS, vS)[t // 2][:, bass.ds(i * 2 + t % 2, 1), :].rearrange("p a t -> p (a t)"),
                       psum[:, t % 2, NPR:T], ACT.Copy).then_inc(sem("p_free"), 1)
                act.wait_ge(sem("p_free"), val(i, 4, M_KV + 4 + 2))
                act.sem_inc(sem("kv_out"), 1)
                for n, name in enumerate(("fk", "fv")):
                    act.dma_start(O[name][:, bass.ds(i * (2 * T), 2 * T)],
                                  kvp[:, 2 * n:2 * n + 2, :].rearrange("p a t -> p (a t)")).then_inc(sem("stored_kv"), 16)
                act.wait_ge(sem("vr_t"), val(i, 1, 1))
                act.wait_ge(sem("at_y"), val(i, 2, MH))
                ac(vrow, B.rearrange("p (h t n) -> p h t n", h=2, t=NT), ACT.Copy).then_inc(sem("vr_out"), 1)
                for j in range(2):
                    attend_prompt(i * 2 + (MH + j), True, oT[:, bass.ds(i * 2 + j, 1), 0:NPR].rearrange("p a t -> p (a t)"))
            attend_sample("fs", FH, PAGES, None, 1, 0)
            with act.Fori(1, NS) as s:
                attend_sample("fs", FH, PAGES, s, 1, 0)
            memory_samples(0)
            with act.Fori(0, 4) as i:
                for t in range(4):
                    tile_out(i, 4, M_G0 + t, dyn(gT, i * 4, t), T, func=ACT.Silu)
            act.wait_ge(sem("u_out"), 1)
            with act.Fori(0, 4) as i:
                for t in range(4):
                    tile_out(i, 4, M_WO0 + t, dyn(oT, i * 4, t), T)
            root(2, rs)
            act.wait_ge(sem("stored_kv"), after(32 * FH // 2))
            memory(1)
            root(4, rs)
            act.wait_ge(sem("lr_free"), 1)
            for t in range(2):
                tile_out(None, 2, M_LORA + t, pb[0:LORA, t, 1:T + 1], T, width=LORA)
            act.wait_ge(sem("lr_s"), 1)
            ac(wlT[0:LORA, 0, :], sx[0:LORA, 0, :], ACT.Tanh)
            ac(wlT[0:LORA, 1, :], sx[0:LORA, 1, :], ACT.Copy).then_inc(sem("lr_out"), 1)
            for t in range(4):
                tile_out(None, 4, M_QM1 + t, qT1[:, t, :], T, scale=SCALE)
            for h in range(MH):
                attend_prompt(MH + FH + h, False, oT[:, FH + h, 0:NPR])
            memory_samples(1)
            with act.Fori(0, RP // 2) as i:
                for j in range(2):
                    o = i * 2 + j
                    act.wait_ge(sem("mix"), after(o))
                    for t in range(3):
                        tile_out(i, 6, M_RKV + 3 * j + t, pb[:, t, 1:T + 1], T)
                    v = runit[:, j, OFF_V:OFF_V + 10]
                    act.wait_ge(sem("wa_y"), o + 1)
                    act.wait_ge(sem("pair_done"), after(o))
                    ac(lw, A[:, 0:T], ACT.Sigmoid, bias=v[:, W0:W0 + 1])
                    ac(aa, Wp[:, 0:T], ACT.Sigmoid, bias=v[:, A0:A0 + 1]).then_inc(sem("wa_out"), 1)
                    act.wait_ge(sem("kk_ss"), o + 1)
                    ac(kk, A[:, 0:T], ACT.Sqrt).then_inc(sem("kk_rt"), 1)
                    act.wait_ge(sem("cum"), o + 1)
                    ac(E1, cc[:, 0:NPR], ACT.Exp)
                    ac(E2, cc[:, 0:NPR], ACT.Exp, scale=-1.0)
                    ac(sc4, sc4, ACT.Exp)
                    ac(bonus[:, 0:NPR], yT[:, 0:NPR], ACT.Exp)
                    ac(lw[:, NPR:T], lw[:, NPR:T], ACT.Exp).then_inc(sem("ex_out"), 1)
                    for c in range(NT):
                        act.wait_ge(sem("rw_t"), o * 2 + (c + 1))
                        ac(rows[:, c, :, :].rearrange("p a t -> p (a t)"), B[:, 0:3 * P], ACT.Copy).then_inc(sem("rw_out"), 1)
                    for n in range(1, LEVELS):
                        act.wait_ge(sem("lv_w"), o * LEVELS + (n + 1))
                        ac(Wsb, Wp, ACT.Copy).then_inc(sem("ws_out"), 1)
                    for c in range(NT):
                        act.wait_ge(sem("c_y"), o * 2 + (c + 1))
                        ac(Cn, Wp[:, 0:P], ACT.Copy, scale=-1.0).then_inc(sem("c_out"), 1)
                        act.wait_ge(sem("sa_y"), o * 2 + (c + 1))
                        ac(SA, Wp[:, P:2 * P], ACT.Copy).then_inc(sem("sa_out"), 1)
                    act.wait_ge(sem("gn_ms"), o + 1)
                    ac(rn, rn, ACT.Sqrt).then_inc(sem("gn_rt"), 1)
                    act.wait_ge(sem("st_out"), o + 1)
                    act.dma_start(O["wp"][bass.ds(o, 1)].rearrange("a p n -> (a p) n"), ST).then_inc(sem("pair_stored_p"), 16)
                    act.wait_ge(sem("ss_out"), o + 1)
                    act.dma_start(O["ws"][bass.ds(o, 1)].rearrange("a p n -> (a p) n"), s0[:, j, :]).then_inc(sem("pair_stored"), 16)
            act.wait_ge(sem("mix"), after(RP))
            act.dma_start(O["sh"], shout[:, :, :].rearrange("p a b -> p (a b)")).then_inc(sem("stored_sh"), 16)
            act.wait_ge(sem("pair_done"), after(RP))
            with act.Fori(0, 4) as i:
                for t in range(4):
                    tile_out(i, 4, M_G1 + t, dyn(gT, i * 4, t), T, func=ACT.Silu)
            act.wait_ge(sem("u_out"), 2)
            with act.Fori(0, 4) as i:
                for t in range(4):
                    tile_out(i, 4, M_WO1 + t, dyn(oT, i * 4, t), T)
            root(5, rs)
            act.wait_ge(sem("x_out"), 2)
            act.dma_start(O["yT"], xT[:, :, :].rearrange("p k t -> p (k t)")).then_inc(sem("stored_y"), 16)
            act.wait_ge(sem("stored_y"), 16)
            act.wait_ge(sem("stored_lf"), 16)
            act.wait_ge(sem("stored_sh"), 16)
            act.wait_ge(sem("stored_kv"), after(32 * FH // 2))
            act.wait_ge(sem("pair_stored"), 16 * RP)
            act.wait_ge(sem("pair_stored_p"), after(16 * RP))

        @block.vector
        def _(dve):
            v_ = nc.vector
            tt, ts, stt = v_.tensor_tensor, v_.tensor_scalar, v_.scalar_tensor_tensor
            ch = Chain(dve, "dve_step")

            def squares(o, dst, src, n):
                for c in range(4):
                    tt(dst[:, 4 * c:4 * c + 4, 0:n], src[:, 4 * c:4 * c + 4, 0:n], src[:, 4 * c:4 * c + 4, 0:n],
                       ALU.mult).then_inc(sem("n_sq"), 1)

            def inverse_root(o, n):
                dve.wait_ge(sem("n_ss"), o + 1)
                ts(rs[:, 0:n], A[:, 0:n], 1.0 / D, RMS_EPS, ALU.mult, ALU.add).then_inc(sem("n_ms"), 1)
                dve.wait_ge(sem("n_rt"), o + 1)
                ch.do(v_.reciprocal(rs[:, 0:n], rs[:, 0:n]))

            def norm(o, dst, src, n, g):
                squares(o, dst, src, n)
                inverse_root(o, n)
                for k in range(KT):
                    last = stt(dst[:, k, 0:n], src[:, k, 0:n], g[:, k:k + 1], rs[:, 0:n], ALU.mult, ALU.mult)
                last.then_inc(sem("n_out"), 1)

            memv = gflat[:, 0:KT * NMEM].rearrange("p (k t) -> p k t", k=KT)

            def attend_prompt(o, causal):
                dve.wait_ge(sem("at_s"), o + 1)
                for t in range(NT):
                    nk = P * (t + 1) if causal else NMEM
                    last = v_.tensor_reduce(nm[:, t:t + 1], X[:, t, 0:nk], AX.X, ALU.max, negate=True)
                last.then_inc(sem("at_m"), 1)
                dve.wait_ge(sem("at_e"), o + 1)
                ch.do(v_.reciprocal(rinv, rsum))
                for t in range(NT):
                    nk = P * (t + 1) if causal else NMEM
                    last = ts(Pp[:, t, 0:nk], Pp[:, t, 0:nk], rinv[:, t:t + 1], None, ALU.mult)
                last.then_inc(sem("at_p"), 1)

            def memory_prompt(base, q):
                for h in range(MH):
                    dve.wait_ge(sem("at_s"), base + h)
                    v_.tensor_copy(qh[:, 0, 0:NPR], q[:, h, 0:NPR]).then_inc(sem("at_in"), 1)
                    attend_prompt(base + h, False)

            def score(x, nh, ng, q, full, page, i, per, o):
                fox = x == "fs"
                tt(qd[:, 0:nh * P].rearrange("p (h n) -> p h n", h=nh), ident.unsqueeze(1).to_broadcast([P, nh, P]),
                   q.to_broadcast([P, nh, P]), ALU.mult).then_inc(sem(x + "_qd"), 1)
                dve.wait_ge(sem(x + "_qbs"), val(i, per, o + 1))
                for g in range(ng):
                    full(g)
                    for h in range(nh):
                        last = v_.tensor_tensor_reduce(page(g, h), page(g, h), qb[:, h * P:(h + 1) * P], 1.0, 0.0,
                                                       ALU.mult, ALU.add, S[:, g * nh + h:g * nh + h + 1])
                    if fox:
                        last.then_inc(sem("k_used"), 1)
                    elif g == ng - 1:
                        last.then_inc(sem("ms_kd"), 1)

            def softmax(x, s, nh, ng, i, per, o):
                g3 = lambda b: b[:, 0:ng * nh].rearrange("p (g h) -> p g h", h=nh)
                bc = lambda b: b[:, 0:nh].unsqueeze(1).to_broadcast([P, ng, nh])
                fox = x == "fs"
                if fox:
                    lfs = lambda g: lf[:, bass.ds(s * (PAGES * FH) + g * FH, FH)]
                    ch.do(v_.memset(Fs[:, (PAGES - 1) * FH:PAGES * FH], 0.0))
                    for g in range(PAGES - 2, -1, -1):
                        ch.do(tt(Fs[:, g * FH:(g + 1) * FH], Fs[:, (g + 1) * FH:(g + 2) * FH], lfs(g + 1), ALU.add))
                    ts(ld[0:FH, :], ident[0:FH, 0:FH], fpT[:, bass.ds(s + NPR, 1)], None, ALU.mult).then_inc(sem(x + "_ld"), 1)
                    dve.wait_ge(sem(x + "_b"), val(i, per, o + 1))
                    dve.wait_ge(sem("k_used"), s * PAGES + PAGES)
                    ch.do(tt(S, S, A[:, 0:ng * nh], ALU.add))
                else:
                    dve.wait_ge(sem("ms_kd"), val(i, per, o + 1))
                v_.tensor_reduce(mx[:, 0:nh], S[:, 0:ng * nh].rearrange("p (g h) -> p h g", h=nh), AX.X, ALU.max)\
                    .then_inc(sem(x + "_mx"), 1)
                dve.wait_ge(sem(x + "_mt"), val(i, per, o + 1))
                ch.do(v_.tensor_reduce(m12[0:nh, :], B[0:nh, 0:P], AX.X, ALU.max))
                ts(dg[0:nh, 0:nh], ident[0:nh, 0:nh], m12[0:nh, 0:1], None, ALU.mult).then_inc(sem(x + "_dg"), 1)
                dve.wait_ge(sem(x + "_mb"), val(i, per, o + 1))
                if fox:
                    me = selfS[:, :, bass.ds(s, 1)].rearrange("p h a -> p (h a)")
                    ch.do(tt(mb[:, 0:nh], A[:, 256:256 + nh], me, ALU.max))
                    tt(pse, me, mb, ALU.subtract)
                else:
                    ch.do(v_.tensor_copy(mb[:, 0:nh], A[:, 256:256 + nh]))
                if fox:
                    dve.wait_ge(sem(x + "_dg"), val(i, per, o + 1))
                tt(g3(S), g3(S), bc(mb), ALU.subtract).then_inc(sem(x + "_sub"), 1)
                dve.wait_ge(sem(x + "_e"), val(i, per, o + 1))
                v_.tensor_reduce(ps[:, 0:nh], Ps[:, 0:ng * nh].rearrange("p (g h) -> p h g", h=nh), AX.X, ALU.add)\
                    .then_inc(sem(x + "_ps"), 1)
                dve.wait_ge(sem(x + "_den"), val(i, per, o + 1))
                if fox:
                    ch.do(tt(rden[:, 0:nh], A[:, 256:256 + nh], pse[:, 0:nh], ALU.add))
                    ch.do(v_.reciprocal(rden[:, 0:nh], rden[:, 0:nh]))
                    ch.do(tt(osum, vS[:, :, bass.ds(s, 1)].rearrange("p h a -> p (h a)"), pse, ALU.mult))
                else:
                    ch.do(v_.reciprocal(rden[:, 0:nh], A[:, 256:256 + nh]))

            def finish(x, s, nh, out, i, per, o):
                if x == "fs":
                    dve.wait_ge(sem("v_used"), s * PAGES + PAGES)
                    ch.do(tt(osum, osum, Y[:, 0:nh], ALU.add))
                    ch.do(tt(out, osum[:, 0:nh].unsqueeze(2), rden[:, 0:nh].unsqueeze(2), ALU.mult))
                else:
                    dve.wait_ge(sem("ms_pv"), val(i, per, o + 1))
                    tt(out, Y[:, 0:nh].unsqueeze(2), rden[:, 0:nh].unsqueeze(2), ALU.mult).then_inc(sem("ms_free"), 1)

            def memory_samples(layer, q):
                with dve.Fori(0, NS // 2) as i:
                    ch.enter(i, 2 * 3)
                    for j in range(2):
                        s = i * 2 + (NPR + j)
                        score("ms", MH, 2, q[:, :, bass.ds(s, 1)],
                              lambda g: dve.wait_ge(sem(f"mk_full{j}"), val(i, 16, 16 * (layer * NS // 2 + 1))),
                              lambda g, h: kring[:, j, g * 512 + h * P:g * 512 + (h + 1) * P], i, 2, layer * NS + j)
                        softmax("ms", None, MH, 2, i, 2, layer * NS + j)
                        finish("ms", None, MH, oT[:, FH:KT, bass.ds(s, 1)], i, 2, layer * NS + j)
                    ch.leave(NS // 2)

            def gated(n, samples):
                dve.wait_ge(sem("ms_free"), samples + 2)
                dve.wait_ge(sem("p_free"), n)
                for c in range(4):
                    last = tt(gT[:, 4 * c:4 * c + 4, :], oT[:, 4 * c:4 * c + 4, :], gT[:, 4 * c:4 * c + 4, :], ALU.mult)
                last.then_inc(sem("u_out"), 1)

            def residual(o, n, layer):
                dve.wait_ge(sem("p_free"), n)
                squares(o, hT, oT, T)
                inverse_root(o, T)
                g = gpost(layer)
                for k in range(KT):
                    last = stt(oT[:, k, :], oT[:, k, :], g[:, k:k + 1], rs, ALU.mult, ALU.mult)
                ch.do(last)
                for c in range(4):
                    last = tt(xT[:, 4 * c:4 * c + 4, :], xT[:, 4 * c:4 * c + 4, :], oT[:, 4 * c:4 * c + 4, :], ALU.add)
                ch.do(last)
                dve.sem_inc(sem("n_out"), 1)
                dve.sem_inc(sem("x_out"), 1)

            for name in ahead:
                dve.sem_inc(sem(name), 1)
            dve.sem_inc(sem("ms_free"), 2)
            dve.wait_ge(sem("const_in"), 16)
            dve.wait_ge(sem("vec_in"), 16)
            dve.wait_ge(sem("mem_in0"), 16)
            norm(0, oT, memv, NMEM, gmem(0))
            dve.wait_ge(sem("x_in"), 16)
            norm(1, hT, xT, T, gpre(0))
            dve.wait_ge(sem("vec_in2"), 16)
            dve.wait_ge(sem("f_y"), 1)
            ch.do(ts(fpT, A[0:FH, 0:T], bf[:, 0:1], None, ALU.add))
            ch.do(ts(ftmp, fpT, -1.0, None, ALU.mult))
            tt(ftmp, ftmp, fpT, ALU.max).then_inc(sem("f_abs"), 1)
            ch.do(ts(fpT, fpT, 0.0, None, ALU.min))
            dve.wait_ge(sem("f_ln"), 1)
            tt(fpT, fpT, ftmp, ALU.subtract).then_inc(sem("f_out"), 1)
            dve.wait_ge(sem("p_free"), M_QM0 + 4 + 2)
            dve.wait_ge(sem("mr_out"), MH)
            memory_prompt(0, qT[:, FH:KT, :])
            dve.wait_ge(sem("d_out"), 1)
            dve.wait_ge(sem("f_out"), 1)
            with dve.Fori(0, FH // 2) as i:
                ch.enter(i, 2)
                dve.wait_ge(sem("at_s"), val(i, 2, MH))
                v_.tensor_copy(qh[:, :, 0:NPR], qT[:, bass.ds(i * 2, 2), 0:NPR])
                for j in range(2):
                    dve.wait_ge(sem("at_s"), val(i, 2, MH + j))
                    sel = ident[0:FH, bass.ds(i * 2 + j, 1)]
                    ts(dm[:, 0, :], dT, sel, None, ALU.mult)
                    ts(dm[:, 1, :], dT, sel, -1.0, ALU.mult, ALU.mult).then_inc(sem("at_in"), 1)
                    attend_prompt(i * 2 + (MH + j), True)
                dve.wait_ge(sem("at_s"), val(i, 2, MH + 2))
                dve.wait_ge(sem("at_in"), val(i, 2, MH + 2))
                dve.sem_inc(sem("kv_free"), 1)
                ch.leave(FH // 2)
            dve.wait_ge(sem("p_free"), M_KV + 24 + 2)
            dve.wait_ge(sem("at_o"), MH + FH)
            tt(prod[:, 0:FH * NS].rearrange("p (h s) -> p h s", h=FH), qT[:, 0:FH, NPR:T], kS, ALU.mult).then_inc(sem("self_p"), 1)
            dve.wait_ge(sem("self_y"), 1)
            v_.tensor_copy(selfS.rearrange("p h s -> p (h s)"), A[:, 0:FH * NS]).then_inc(sem("self_out"), 1)
            dve.wait_ge(sem("self_out"), 1)
            def column(buf, s):
                return buf[:, 0:FH, NPR + s:NPR + s + 1] if isinstance(s, int) else buf[:, 0:FH, bass.ds(s + NPR, 1)]

            def pages(s, i):
                score("fs", FH, PAGES, column(qT, s),
                      lambda g: dve.wait_ge(sem(f"k_full{g % KRING}"), s * (32 * PAGES // KRING) + 32 * (g // KRING + 1)),
                      lambda g, h: kring[:, g % KRING, h * P:(h + 1) * P], i, 1, 0)

            pages(0, None)
            softmax("fs", 0, FH, PAGES, None, 1, 0)
            with dve.Fori(1, NS) as s:
                ch.enter(s - 1, 24)
                pages(s, s)
                finish("fs", s - 1, FH, column(oT, s - 1), s, 1, 0)
                softmax("fs", s, FH, PAGES, s, 1, 0)
                ch.leave(NS - 1)
            finish("fs", NS - 1, FH, column(oT, NS - 1), None, 1, 0)
            memory_samples(0, qT[:, FH:KT, :])
            gated(M_G0 + 16 + 2, NS)
            residual(2, M_WO0 + 16 + 2, 0)
            dve.wait_ge(sem("mem_in1"), 16)
            norm(3, oT, memv, NMEM, gmem(1))
            norm(4, hT, xT, T, gpre(1))
            for n in range(3, 5):
                dve.wait_ge(sem(f"vec_in{n}"), 16)
            ch.do(v_.memset(pb[:, :, 0:1], 0.0))
            dve.sem_inc(sem("lr_free"), 1)

            def shift(x, rows_, prev, mu, dst):
                cur = pb[0:rows_, x, 1:T + 1]
                tt(df[0:rows_, 0:NPR], pb[0:rows_, x, 0:NPR], cur[:, 0:NPR], ALU.subtract)
                ch.do(tt(df[0:rows_, NPR:T], prev, cur[:, NPR:T], ALU.subtract))
                ch.do(stt(sx[0:rows_, x, :], df[0:rows_, :], mu, cur, ALU.mult, ALU.add))
                return v_.tensor_copy(dst, pb[0:rows_, x, NPR:T + 1])

            dve.wait_ge(sem("p_free"), M_LORA + 2 + 2)
            v_.memset(shout[:, SHT - 2:SHT, :], 0.0)
            for x in range(2):
                last = shift(x, LORA, shL[0:LORA, x, :], muL[0:LORA, x:x + 1], shout[0:LORA, SHT - 2 + x, :])
            last.then_inc(sem("lr_s"), 1)
            dve.wait_ge(sem("lr_out"), 1)
            dve.wait_ge(sem("p_free"), M_QM1 + 4 + 2)
            dve.wait_ge(sem("mr_out"), 2 * MH)
            memory_prompt(MH + FH, qT1)
            dve.wait_ge(sem("at_o"), 2 * MH + FH)
            memory_samples(1, qT1)
            ch.do(v_.memset(pb[:, :, 0:1], 0.0))
            ch.do(v_.memset(S0p, 0.0))

            with dve.Fori(0, RP // 2) as i:
                ch.enter(i, 68)
                for j in range(2):
                    o = i * 2 + j
                    vec = runit[:, j, OFF_V:OFF_V + 10]
                    col = lambda n: vec[:, n:n + 1]
                    dve.wait_ge(sem(f"r_full{j}"), val(i, 16, 16))
                    dve.wait_ge(sem(f"s0_full{j}"), val(i, 16, 16))
                    dve.wait_ge(sem("p_free"), val(i, 6, M_RKV + 3 * j + 3 + 2))
                    for x in range(3):
                        last = shift(x, P, runit[:, j, OFF_SH + x * NS:OFF_SH + (x + 1) * NS], col(MU_R + x),
                                     shout[:, bass.ds(o * 3 + x, 1), :].rearrange("p a t -> p (a t)"))
                    last.then_inc(sem("mix"), 1)
                    r, k, v = (sx[:, x, :] for x in range(3))
                    dve.wait_ge(sem("mix"), after(o + 1))
                    ch.do(ts(kkr, k, col(K_K), None, ALU.mult))
                    tt(df, kkr, kkr, ALU.mult).then_inc(sem("kk_sq"), 1)
                    dve.wait_ge(sem("wa_out"), o + 1)
                    ch.do(ts(km, aa, 1.0, col(K_A), ALU.subtract, ALU.mult))
                    ch.do(stt(km, km, 1.0, k, ALU.add, ALU.mult))
                    stt(rn, r, col(R_K), km, ALU.mult, ALU.mult).then_inc(sem("rk_p"), 1)
                    ch.do(ts(lw, lw, -EXPM, None, ALU.mult))
                    for c in range(4):
                        last = v_.tensor_tensor_scan(cc[:, c * 64:c * 64 + 64], cst[:, C_ONE:C_ONE + 64], lw[:, c * 64:c * 64 + 64],
                                                     0.0, ALU.mult, ALU.add)
                    ch.do(last)
                    ends = cc[:, 0:NPR].rearrange("p (a t) -> p a t", a=4)[:, :, 63]
                    v_.tensor_copy(sc4, ends)
                    ch.do(v_.tensor_copy(hs4, ends))
                    for c in range(NT):
                        last = ts(cc[:, c * P:c * P + 64], cc[:, c * P:c * P + 64], hs4[:, 2 * c:2 * c + 1], None, ALU.subtract)
                    ch.do(last)
                    tt(yT[:, 0:NPR], cc[:, 0:NPR], lw[:, 0:NPR], ALU.subtract).then_inc(sem("cum"), 1)
                    dve.wait_ge(sem("kk_rt"), o + 1)
                    ch.do(ts(kk, kk, 1e-12, None, ALU.max))
                    ch.do(v_.reciprocal(kk, kk))
                    ch.do(tt(kk, kkr, kk, ALU.mult))
                    ch.do(tt(bb, kk, aa, ALU.mult))
                    dve.wait_ge(sem("ex_out"), o + 1)
                    c3 = lambda b: b[:, 0:NPR].rearrange("p (c t) -> p c t", c=NT)
                    tt(KR[:, :, 0, :], c3(kk), c3(bonus), ALU.mult)
                    tt(KR[:, :, 1, :], c3(r), c3(E1), ALU.mult)
                    tt(bt, bb[:, 0:NPR], E2, ALU.mult)
                    tt(kt, km[:, 0:NPR], E2, ALU.mult).then_inc(sem("tl_in"), 1)
                    dve.wait_ge(sem("tl_in"), o + 1)
                    dve.wait_ge(sem("rk_y"), o + 1)
                    ch.do(tt(bonus, Wp[:, 0:T], v, ALU.mult))
                    for q in range(4):
                        dve.wait_ge(sem("gm_y"), o * 4 + (q + 1))
                        tt(GM[:, q, :], X[:, q % 2, :], cst[:, C_RM:C_RM + 512], ALU.mult).then_inc(sem("gm_out"), 1)
                    dve.wait_ge(sem("gm_out"), after(o * 4 + 4))
                    idb = ident.unsqueeze(1).to_broadcast([P, 4, P])
                    for n in range(LEVELS):
                        if n:
                            dve.wait_ge(sem("lv_w"), o * LEVELS + n)
                        lm = cst[:, C_LM + n * P:C_LM + (n + 1) * P].unsqueeze(1).to_broadcast([P, 4, P])
                        tt(NM, GM[:, :, 0:P], lm, ALU.mult).then_inc(sem("nm_out"), 1)
                        if n == 0:
                            dve.wait_ge(sem("nm_out"), o * LEVELS + 1)
                            tt(TU[:, :, P:2 * P], idb, NM, ALU.subtract)
                            dve.wait_ge(sem("lv_w"), o * LEVELS + 1)
                            tt(TU[:, :, 0:P], idb, Wp.rearrange("p (q t) -> p q t", q=4), ALU.subtract).then_inc(sem("tu_out"), 1)
                            dve.wait_ge(sem("tu_out"), o * LEVELS + 1)
                        else:
                            dve.wait_ge(sem("lv_d"), o * (LEVELS - 1) + n)
                            tt(TU, TU, X.rearrange("p b (q n) -> p (b q) n", q=2), ALU.subtract).then_inc(sem("tu_out"), 1)
                            dve.wait_ge(sem("tu_out"), o * LEVELS + n + 1)
                    for c in range(NT):
                        dve.wait_ge(sem("y_y"), o * 2 + (c + 1))
                        v_.tensor_copy(yT[:, c * P:(c + 1) * P], Y[:, 0:P])
                        if c == 0:
                            dve.wait_ge(sem("pair_stored_p"), after(o * 16))
                            ch.do(ts(ST, Y[:, 128:192], sc4[:, 1:2], None, ALU.mult))
                            ts(S0p[0:64, 0:64], ST[0:64, :], sc4[0:64, 2:3], None, ALU.mult)
                            ch.do(ts(S0p[64:P, 64:P], ST[64:P, :], sc4[64:P, 2:3], None, ALU.mult))
                            dve.sem_inc(sem("st_in"), 1)
                        else:
                            ch.do(stt(ST, ST, sc4[:, 2:3], Y[:, 128:192], ALU.mult, ALU.add))
                            ch.do(ts(ST, ST, sc4[:, 3:4], None, ALU.mult))
                            dve.sem_inc(sem("st_out"), 1)
                        dve.sem_inc(sem("y_out"), 1)
                    s3 = s0[:, j, :].rearrange("p (s v) -> p s v", s=NS)
                    z3 = lambda n: Z[:, n, :].rearrange("p (s v) -> p s v", s=NS)
                    bs = lambda b: b[:, NPR:T].unsqueeze(2).to_broadcast([P, NS, 64])
                    i64 = cst[:, C_I64:C_I64 + 64].unsqueeze(1).to_broadcast([P, NS, 64])
                    tt(z3(0), s3, bs(kk), ALU.mult).then_inc(sem("z_in"), 1)
                    tt(z3(1), i64, bs(v), ALU.mult).then_inc(sem("z_in"), 1)
                    ch.do(tt(s3, s3, bs(lw), ALU.mult))
                    x3 = lambda b: b.rearrange("p (s v) -> p s v", s=NS)
                    dve.wait_ge(sem("z_y"), o * 3 + 1)
                    ch.do(tt(z3(3), x3(X[:, 0, :]), bs(bb), ALU.mult))
                    ch.do(tt(s3, s3, z3(3), ALU.subtract))
                    dve.wait_ge(sem("z_y"), o * 3 + 2)
                    ch.do(tt(z3(3), x3(X[:, 1, :]), bs(km), ALU.mult))
                    tt(s3, s3, z3(3), ALU.add).then_inc(sem("ss_out"), 1)
                    dve.wait_ge(sem("ss_out"), o + 1)
                    tt(z3(2), s3, bs(r), ALU.mult).then_inc(sem("z_in"), 1)
                    dve.wait_ge(sem("z_y"), o * 3 + 3)
                    ch.do(tt(z3(3), x3(Wp), i64, ALU.mult))
                    ch.do(v_.tensor_reduce(yT[:, NPR:T], z3(3), AX.X, ALU.add))
                    dve.sem_inc(sem("gn_in"), 1)
                    dve.wait_ge(sem("gn_y"), o * 2 + 1)
                    ch.do(stt(yT, A[:, 0:T], -1.0 / 64, yT, ALU.mult, ALU.add))
                    ch.do(tt(df, yT, yT, ALU.mult))
                    dve.sem_inc(sem("gn_in"), 1)
                    dve.wait_ge(sem("gn_y"), o * 2 + 2)
                    ch.do(ts(rn, A[:, 0:T], 1.0 / 64, GN_EPS, ALU.mult, ALU.add))
                    dve.sem_inc(sem("gn_ms"), 1)
                    dve.wait_ge(sem("gn_rt"), o + 1)
                    ch.do(v_.reciprocal(rn, rn))
                    ch.do(stt(yT, yT, col(LN_W), rn, ALU.mult, ALU.mult))
                    ch.do(stt(oT[:, bass.ds(o, 1), :].rearrange("p a t -> p (a t)"), yT, col(LN_B), bonus, ALU.add, ALU.add))
                    dve.wait_ge(sem("pair_stored"), o * 16 + 16)
                    dve.sem_inc(sem("pair_done"), 1)
                ch.leave(RP // 2)
            gated(M_G1 + 16 + 2, 2 * NS)
            residual(5, M_WO1 + 16 + 2, 1)


_OUTS = {"yT": (P, KT * T), "mk": (2, P, MH * NMEM), "mv": (2, P, MH * NMEM), "fk": (P, FH * T), "fv": (P, FH * T),
         "lf": (FH, T), "sh": (P, SHT * 9), "wp": (RP, P, 64), "ws": (RP, P, NS * 64)}


def kernel(**inputs):
    import concourse.bacc as bacc
    from concourse.bass_utils import run_bass_kernel_spmd as run

    x = {k: np.asarray(v) for k, v in inputs.items()}

    def tiles(a):
        return a.reshape(-1, P, a.shape[1]).transpose(1, 0, 2)

    def units(w, cols=U):
        n = w.shape[1] // cols
        return w.reshape(KT, P, n, cols).transpose(2, 1, 0, 3).reshape(n, P, KT * cols)

    def columns(a):
        return a.reshape(-1, P).T

    A_ = {}
    A_["consts"] = shape_constants()
    A_["xT"] = tiles(np.concatenate([x["x_prompt"][0], x["x_sample"][:, 0]], 0).T)
    A_["memT"] = tiles(x["mem_prompt"][0].T)
    A_["gvec"] = np.concatenate([columns(x[n][l]) for n in ("g_pre", "g_post", "g_mem") for l in range(2)], 1)
    A_["bf"] = x["fox_b_f"][0][:, None]
    w = x["fox_w_in"][0]
    tw = FH * P
    A_["wq"] = units(w[:, :tw])
    A_["wkv"] = np.stack([units(w[:, tw:2 * tw]), units(w[:, 2 * tw:3 * tw])], 1).reshape(12, P, KT * U)
    A_["wf"] = tiles(w[:, 3 * tw:3 * tw + FH])
    at = 3 * tw + FH
    A_["wqm0"] = units(w[:, at:at + MH * P])
    A_["wg0"] = units(w[:, at + MH * P:])
    for l in range(2):
        A_[f"wo{l}"] = units(x["w_o"][l])
        A_[f"wm{l}"] = units(x["w_mem"][l])
    w = x["rwkv_w_in"][0]
    at = 3 * tw + 2 * LORA
    A_["wl"] = units(w[:, 3 * tw:at], LORA)
    A_["wqm1"] = units(w[:, at:at + MH * P])
    A_["wg1"] = units(w[:, at + MH * P:])
    mu, sh = x["rwkv_mu"][0], x["state_rwkv_shift"][0][:, 0]
    rkv = w[:, :3 * tw].reshape(KT, P, 3, RP, P).transpose(3, 1, 0, 2, 4).reshape(RP, P, KT * RW)

    def lora(a):
        a = a.reshape(LORA, RP, P).transpose(1, 0, 2)
        return np.concatenate([a, np.zeros((RP, P - LORA, P), np.float32)], 1)

    vecs = [mu[:tw], mu[tw:2 * tw], mu[2 * tw:3 * tw]] + [x[n][0] for n in (
        "rwkv_w0", "rwkv_a0", "rwkv_k_k", "rwkv_k_a", "rwkv_r_k", "rwkv_ln_w", "rwkv_ln_b")]
    vecs = np.stack(vecs, 1).reshape(RP, P, 10)
    shift = sh[:, :3 * tw].reshape(NS, 3, RP, P).transpose(2, 3, 1, 0).reshape(RP, P, 3 * NS)
    A_["wrkv"] = np.concatenate([rkv, lora(x["rwkv_w_w2"][0]), lora(x["rwkv_w_a2"][0]), vecs, shift], 2)

    def padded(a):
        return np.concatenate([a, np.zeros((P - LORA,) + a.shape[1:], np.float32)], 0)

    A_["muL"] = padded(mu[3 * tw:].reshape(2, LORA).T)
    A_["shL"] = padded(sh[:, 3 * tw:].reshape(NS, 2, LORA).transpose(2, 1, 0))
    A_["s0"] = x["state_rwkv_wkv"][0].reshape(NS, RP, 2, 64, 64).transpose(1, 2, 4, 0, 3).reshape(RP, P, NS * 64)
    A_["ck"] = x["cache_fox_k"][0].reshape(-1, P, PAGE_W)
    A_["cv"] = x["cache_fox_v"][0].reshape(-1, P, PAGE_W)
    A_["cf"] = x["cache_fox_logf"][0]
    A_["cmk"] = x["cache_mem_k"].reshape(2 * NS, NMEM, MH * P)
    A_["cmv"] = x["cache_mem_v"].reshape(2 * NS, NMEM, MH * P)
    A_["pt"] = x["page_table"].reshape(-1)

    nc = bacc.Bacc("TRN2", target_bir_lowering=False, num_devices=1)
    arrays, I, O = {}, {}, {}
    for n, a in A_.items():
        a = np.ascontiguousarray(a)
        arrays["in_" + n] = a
        I[n] = nc.dram_tensor("in_" + n, a.shape, mybir.dt.from_np(a.dtype), kind="ExternalInput").ap()
    for n, shape in _OUTS.items():
        O[n] = nc.dram_tensor("out_" + n, shape, F32, kind="ExternalOutput").ap()
    trunk_step(nc, I, O)
    res = run(nc, [arrays], core_ids=[0]).results[0]
    o = {n: res["out_" + n] for n in _OUTS}

    y = o["yT"].reshape(P, KT, T).transpose(2, 1, 0).reshape(T, D)
    mem = [o[n].reshape(2, P, MH, NMEM).transpose(0, 3, 2, 1)[:, None] for n in ("mk", "mv")]
    fox = [o[n].reshape(P, FH, T).transpose(2, 1, 0) for n in ("fk", "fv")]
    lf = o["lf"].T
    sh = o["sh"].reshape(P, SHT, 9).transpose(2, 1, 0)
    main = sh[:, :3 * RP].reshape(9, RP, 3, P).transpose(0, 2, 1, 3).reshape(9, 3 * tw)
    sh = np.concatenate([main, sh[:, 3 * RP, :LORA], sh[:, 3 * RP + 1, :LORA]], 1)
    wp = o["wp"].reshape(RP, 2, 64, 64).transpose(0, 1, 3, 2).reshape(1, 1, 2 * RP, 64, 64)
    ws = o["ws"].reshape(RP, 2, 64, NS, 64).transpose(3, 0, 1, 4, 2).reshape(1, NS, 2 * RP, 64, 64)
    out = (y[None, :NPR], y[NPR:, None], mem[0], mem[1],
           fox[0][None, None, :NPR], fox[1][None, None, :NPR], lf[None, None, :NPR],
           fox[0][None, NPR:, None], fox[1][None, NPR:, None], lf[None, NPR:, None],
           wp, sh[None, None, 0:1], ws, sh[None, 1:, None])
    return tuple(np.ascontiguousarray(a) for a in out)
```

```python
from contextlib import ExitStack

import numpy as np

import concourse.bass as bass
from concourse import mybir

F32 = mybir.dt.float32
I32 = mybir.dt.int32
ALU = mybir.AluOpType
ACT = mybir.ActivationFunctionType
AX = mybir.AxisListType

P = 128
D = 2048
KT = D // P
NPR = 256
NS = 8
T = NPR + NS
NT = NPR // P
FH = 12
MH = 4
NMEM = 256
PAGES = 16
PAGE_W = FH * 128
RP = 12
LORA = 96
SHT = 38
U = 256
RW = 3 * P
RUNIT = KT * RW
OFF_A2 = P
OFF_V = 2 * P
OFF_SH = OFF_V + 8
VUNIT = OFF_SH + 3 * NS
KRING = 4
VRING = 4
AR = 11500
SCALE = 128.0 ** -0.5
EXPM = float(np.exp(-0.5))
RMS_EPS = 1e-6
GN_EPS = 64e-5
LEVELS = 7
MU_R, MU_K, MU_V, W0, A0, K_K, K_A, R_K = range(8)

C_ID, C_ONE, C_BO, C_TRI, C_CAUS = 0, 128, 384, 512, 640
C_I64 = 768
C_N = C_I64 + 64
K_RM, K_LM = 0, 512
K_N = K_LM + LEVELS * 128


def shape_constants():
    s = np.arange(P)[:, None]
    t = np.arange(P)[None, :]
    c = np.zeros((P, C_N), np.float32)
    c[:, C_ID:C_ID + P] = s == t
    c[:, C_ONE:C_ONE + 256] = 1.0
    c[:, C_BO:C_BO + P] = s // 64 == t // 64
    c[:, C_TRI:C_TRI + P] = s > t
    c[:, C_CAUS:C_CAUS + P] = np.where(t <= s, 0.0, -1e30)
    c[:, C_I64:C_I64 + 64] = s % 64 == np.arange(64)[None, :]
    k = np.zeros((P, K_N), np.float32)
    for n in range(4):
        k[:, K_RM + n * P:K_RM + (n + 1) * P] = (s < t) if n % 2 == 0 else (s <= t)
    for n in range(LEVELS):
        m = 2 ** n
        k[:, K_LM + n * P:K_LM + (n + 1) * P] = (s // (2 * m) == t // (2 * m)) & (s % (2 * m) < m) & (t % (2 * m) >= m)
    return c, k


M_MEM = (0, 80)
M_Q, M_QM0, M_KV, M_G0, M_WO0 = 8, 20, 24, 48, 64
M_LORA, M_QM1, M_RKV, M_G1, M_WO1 = 88, 90, 94, 130, 146
U_MEM = (0, 40)
U_Q, U_QM0, U_KV, U_G0, U_WO0 = 4, 10, 12, 24, 32
U_LORA, U_QM1, U_G1, U_WO1 = 44, 46, 48, 56


def trunk_step(nc, I, O):
    ctx = ExitStack()
    with ctx:
        def sb(name, shape, dt=F32):
            return ctx.enter_context(nc.sbuf_tensor(name, shape, dt))

        sems = {}

        def sem(name):
            if name not in sems:
                sems[name] = ctx.enter_context(nc.semaphore(name))
            return sems[name]

        xT = sb("xT", [P, KT, T])
        hT = sb("hT", [P, KT, T])
        oT = sb("oT", [P, KT, T])
        gT = sb("gT", [P, KT, T])
        wring = sb("wring", [P, 2, KT * U])
        kvr = sb("kvr", [P, 2 * (RUNIT + VUNIT)])
        cst = sb("cst", [P, C_N])
        kmT = sb("kmT", [P, MH, NMEM])
        vmr = sb("vmr", [P, NT, MH, P])
        gvec = sb("gvec", [P, 3, 2, KT])
        lnv = sb("lnv", [P, RP, 2])
        muL = sb("muL", [P, 2])
        shL = sb("shL", [P, 2, NS])
        shout = sb("shout", [P, SHT, 1 + NS])
        bf = sb("bf", [FH, 1])
        pts = sb("pts", [1, NS * PAGES], I32)
        arena = sb("arena", [P, AR])

        class Region:
            def __init__(self, ap, size):
                self.ap, self.size, self.at = ap, size, 0

            def take(self, *shape, parts=P):
                n = int(np.prod(shape))
                a = self.ap[0:parts, self.at:self.at + n]
                self.at += n
                assert self.at <= self.size, (self.at, self.size)
                if len(shape) == 1:
                    return a
                names = "abcd"[:len(shape)]
                return a.rearrange(f"p ({' '.join(names)}) -> p {' '.join(names)}",
                                   **{x: s for x, s in zip(names, shape)})

        psum = ctx.enter_context(nc.psum_tensor("psum", [P, 8, 512], F32))
        A, B, Wp, Y = (psum[:, n, :] for n in (2, 3, 4, 7))
        X = psum[:, 5:7, :]

        gflat = gT[:, :, :].rearrange("p k t -> p (k t)")
        kring = kvr[:, 0:KRING * PAGE_W].rearrange("p (r n) -> p r n", r=KRING)
        vring = kvr[:, KRING * PAGE_W:(KRING + VRING) * PAGE_W].rearrange("p (r n) -> p r n", r=VRING)
        runit = kvr[:, 0:2 * RUNIT].rearrange("p (r n) -> p r n", r=2)
        vunit = kvr[:, 2 * RUNIT:].rearrange("p (r n) -> p r n", r=2)
        ident = cst[:, C_ID:C_ID + P]
        ones = cst[:, C_ONE:C_ONE + P]
        blockones = cst[:, C_BO:C_BO + P]

        r0 = Region(arena, AR)
        qT = r0.take(KT, T)
        kvp = r0.take(4, T)
        lf = r0.take(NS * PAGES * FH)
        fpT = r0.take(T, parts=FH)
        frow = r0.take(NT, FH)
        dT = r0.take(NPR, parts=FH)
        ftmp = r0.take(T, parts=FH)
        kS = r0.take(FH, NS)
        vS = r0.take(FH, NS)
        selfS = r0.take(FH, NS)
        rs = r0.take(T)
        wfb = r0.take(KT, FH)
        base0 = r0.at
        qh = r0.take(2, T)
        dm = r0.take(2, NPR, parts=FH)
        vrow = r0.take(2, NT, P)
        nm = r0.take(2)
        rsum = r0.take(2)
        rinv = r0.take(2)
        rg = Region(gflat, KT * T)
        qd = rg.take(FH * P)
        qb = rg.take(FH * P)
        Pp = rg.take(2, NPR)
        PT = rg.take(2, NPR)
        r0.at = base0
        S = r0.take(PAGES * FH)
        Ps = r0.take(PAGES * FH)
        Fs = r0.take(PAGES * FH)
        mx = r0.take(FH)
        m12 = r0.take(1)
        dg = r0.take(FH)
        ld = r0.take(FH)
        mb = r0.take(FH)
        pse = r0.take(FH)
        ps = r0.take(FH)
        rden = r0.take(FH)
        osum = r0.take(FH)
        prod = r0.take(P)

        r1 = Region(arena, AR)
        qT1 = r1.take(MH, T)
        wlT = r1.take(2, T)
        pb = r1.take(2, 3, T + 1)
        sx = r1.take(3, T)
        df = r1.take(T)
        lw = r1.take(T)
        aa = r1.take(T)
        kkr = r1.take(T)
        kk = r1.take(T)
        km = r1.take(T)
        bb = r1.take(T)
        cc = r1.take(T)
        rn = r1.take(T)
        bonus = r1.take(2, T)
        grn = r1.take(T)
        E1 = r1.take(NPR)
        E2 = r1.take(NPR)
        E3 = r1.take(NPR)
        bt = r1.take(NPR)
        kt = r1.take(NPR)
        s0 = r1.take(2, NS * 64)
        Cn = r1.take(P)
        SA = r1.take(P)
        ST = r1.take(P)
        S0p = r1.take(P)
        sc4 = r1.take(2, 4)
        hs4 = r1.take(4)
        ys = r1.take(2, NS)
        Wsb = r1.take(4 * P)
        rg1 = Region(gflat, KT * T)
        NM = rg1.take(2, 4, P)
        TU = rg1.take(4, 2 * P)
        Z = rg1.take(2, NS * 64)
        yT = rg1.take(T)
        gdf = rg1.take(T)
        rw1 = Region(wring[:, :, :].rearrange("p a n -> p (a n)"), 2 * KT * U)
        masks = rw1.take(K_N)
        KR = rw1.take(2, NT, 2 * P)
        rows = rw1.take(2, NT, 3 * P)
        GM = rw1.take(2, 4, 512)

        gpre = lambda l: gvec[:, 0, l, :]
        gpost = lambda l: gvec[:, 1, l, :]
        gmem = lambda l: gvec[:, 2, l, :]

        def val(i, per, k):
            return k if i is None else i * per + k

        ahead = ("lv_w", "prepared", "stored_kv", "kv_free", "pair_done", "mix", "rw_out", "gm_out", "pair_stored_p", "y_out")

        def after(n):
            return n + 1

        class Chain:

            def __init__(self, eng, name):
                self.eng, self.s, self.n, self.i, self.per = eng, sem(name), 0, None, 0

            def do(self, ins):
                self.n += 1
                ins.then_inc(self.s, 1)
                self.eng.wait_ge(self.s, val(self.i, self.per, self.n))

            def enter(self, i, per):
                self.i, self.per, self.n0 = i, per, self.n

            def leave(self, count):
                assert self.n - self.n0 == self.per, f"{self.n - self.n0} steps an iteration, not {self.per}"
                self.n, self.i = self.n0 + count * self.per, None

        STEPS = 68

        block = ctx.enter_context(nc.Block())

        @block.sync
        def _(sp):
            sp.dma_start(cst[:, :], I["consts"]).then_inc(sem("const_in"), 16)
            sp.dma_start(gflat[:, 0:KT * NMEM], I["memT"].rearrange("p k t -> p (k t)")).then_inc(sem("mem_in0"), 16)
            sp.dma_start(gvec[:, :, :, :].rearrange("p a l k -> p (a l k)"), I["gvec"]).then_inc(sem("vec_in"), 16)
            sp.dma_start(bf[:, :], I["bf"]).then_inc(sem("vec_in2"), 16)
            sp.dma_start(muL[:, :], I["muL"]).then_inc(sem("vec_in3"), 16)
            sp.dma_start(lnv[:, :, :].rearrange("p a b -> p (a b)"), I["lnv"]).then_inc(sem("vec_in5"), 16)
            sp.dma_start(shL[:, :, :], I["shL"]).then_inc(sem("vec_in4"), 16)

            def unit(arr, index, slot):
                dst = wring[:, slot, :]
                if isinstance(index, int):
                    src = arr[index]
                else:
                    src = arr[bass.ds(index, 1)].rearrange("a p n -> (a p) n")
                sp.dma_start(dst[:, 0:src.shape[1]], src).then_inc(sem(f"w_full{slot}"), 16)

            def units(arr, count, m0):
                with sp.Fori(0, count // 2) as i:
                    for j in range(2):
                        index = sp.snap(i * 2 + j)
                        sp.wait_ge(sem("p_done"), val(i, 4, m0 + 2 * j - 2))
                        unit(arr, index, j)

            unit(I["wm0"], 0, 0)
            unit(I["wm0"], 1, 1)
            sp.dma_start(xT[:, :, :], I["xT"]).then_inc(sem("x_in"), 16)
            for n in range(2, 4):
                sp.wait_ge(sem("p_done"), 2 * n - 2)
                unit(I["wm0"], n, n % 2)
            units(I["wq"], 6, M_Q)
            units(I["wqm0"], 2, M_QM0)
            units(I["wkv"], 12, M_KV)
            units(I["wg0"], 8, M_G0)
            units(I["wo0"], 8, M_WO0)
            units(I["wm1"], 4, M_MEM[1])
            sp.wait_ge(sem("p_done"), M_MEM[1] + 8 - 2)
            unit(I["wl"], 0, 0)
            sp.wait_ge(sem("p_done"), M_MEM[1] + 8)
            unit(I["wl"], 1, 1)
            sp.wait_ge(sem("p_done"), M_LORA + 1)
            unit(I["wqm1"], 0, 0)
            sp.wait_ge(sem("p_done"), M_LORA + 2)
            unit(I["wqm1"], 1, 1)

            def pair(index, name, dst, full):
                src = I[name][index] if isinstance(index, int) else I[name][bass.ds(index, 1)].rearrange("a p n -> (a p) n")
                sp.dma_start(dst, src).then_inc(sem(full), 16)

            sp.wait_ge(sem("ms_free"), 2 * NS + 2)
            for j in range(2):
                pair(j, "wrkv", runit[:, j, :], f"r_full{j}")
                pair(j, "vrkv", vunit[:, j, :], f"v1_full{j}")
                pair(j, "s0", s0[:, j, :], f"s0_full{j}")
            sp.wait_ge(sem("p_done"), M_QM1 + 4)
            sp.dma_start(masks, I["masks"]).then_inc(sem("masks_in"), 16)
            with sp.Fori(0, RP // 2 - 1) as i:
                for j in range(2):
                    a, b, c = sp.snap(i * 2 + (2 + j)), sp.snap(i * 2 + (2 + j)), sp.snap(i * 2 + (2 + j))
                    sp.wait_ge(sem("p_done"), val(i, 6, M_RKV + 3 * j + 3))
                    pair(a, "wrkv", runit[:, j, :], f"r_full{j}")
                    sp.wait_ge(sem("prepared"), after(val(i, 2, j + 1)))
                    pair(b, "vrkv", vunit[:, j, :], f"v1_full{j}")
                    sp.wait_ge(sem(f"pair_stored{j}"), val(i, 16, 16))
                    pair(c, "s0", s0[:, j, :], f"s0_full{j}")
            sp.wait_ge(sem("pair_done"), after(RP))
            units(I["wg1"], 8, M_G1)
            units(I["wo1"], 8, M_WO1)

        @block.gpsimd
        def _(pool):
            pool.dma_start(pts[:, :], I["pt"].rearrange("(a b) -> a b", a=1)).then_inc(sem("pt_in"), 16)
            pool.wait_ge(sem("pt_in"), 16)
            npool = I["ck"].shape[0]

            def page_id(s, g):
                return pool.value_load(pts[0:1, bass.ds(s * PAGES + g, 1)], min_val=0, max_val=npool - 1)

            def k_page(s, g, nth):
                if nth is not None:
                    pool.wait_ge(sem("k_used"), nth)
                pid = page_id(s, g)
                pool.dma_start(kring[:, g % KRING, :],
                               I["ck"][bass.ds(pid, 1)].rearrange("a p n -> (a p) n")).then_inc(sem(f"k_full{g % KRING}"), 16)
                pool.dma_start(lf[:, bass.ds((s * PAGES + g) * FH, FH)],
                               I["cf"][bass.ds(pid, 1)].rearrange("a p n -> (a p) n")).then_inc(sem(f"k_full{g % KRING}"), 16)

            def v_page(s, g, nth):
                if nth is not None:
                    pool.wait_ge(sem("v_used"), nth)
                pid = page_id(s, g)
                pool.dma_start(vring[:, g % VRING, :],
                               I["cv"][bass.ds(pid, 1)].rearrange("a p n -> (a p) n")).then_inc(sem(f"v_full{g % VRING}"), 16)

            for g in range(PAGES):
                k_page(0, g, g - KRING + 1 if g >= KRING else None)
            for g in range(PAGES):
                v_page(0, g, g - VRING + 1 if g >= VRING else None)
                k_page(1, g, PAGES + g - KRING + 1)
            with pool.Fori(1, NS - 1) as s:
                for g in range(PAGES):
                    v_page(s, g, s * PAGES + (g - VRING + 1))
                    k_page(s + 1, g, s * PAGES + (PAGES + g - KRING + 1))
            for g in range(PAGES):
                v_page(NS - 1, g, (NS - 1) * PAGES + g - VRING + 1)

            pool.wait_ge(sem("k_used"), NS * PAGES)
            pool.wait_ge(sem("v_used"), NS * PAGES)
            for layer in range(2):
                if layer == 1:
                    pool.wait_ge(sem("p_done"), M_WO0 + 16)
                    pool.dma_start(gflat[:, 0:KT * NMEM], I["memT"].rearrange("p k t -> p (k t)")).then_inc(sem("mem_in1"), 16)
                with pool.Fori(0, NS // 2) as i:
                    for j in range(2):
                        row = i * 2 + (layer * NS + j)
                        pool.wait_ge(sem("ms_free"), val(i, 2, layer * NS + j + 1))
                        for ring, name, full in ((kring, "cmk", "mk_full"), (vring, "cmv", "mv_full")):
                            pool.dma_start(ring[:, j, 0:1024].rearrange("p (t n) -> p t n", t=2),
                                           I[name][bass.ds(row, 1)].rearrange("a (t p) n -> p (a t) n", p=P))\
                                .then_inc(sem(f"{full}{j}"), 16)

            pool.wait_ge(sem("masks_in"), 16)
            with pool.Fori(0, RP // 2) as i:
                for j in range(2):
                    o = i * 2 + j
                    for n in range(LEVELS):
                        if n == 0:
                            pool.wait_ge(sem("gm_out"), after(o * 4 + 4))
                        if n == 2:
                            pool.wait_ge(sem("tu_out"), o * LEVELS + 1)
                        pool.wait_ge(sem("lv_w"), after(o * LEVELS + max(n - 1, 0)))
                        lm = masks[:, K_LM + n * P:K_LM + (n + 1) * P].unsqueeze(1).to_broadcast([P, 4, P])
                        nc.gpsimd.tensor_tensor(NM[:, n % 2, :, :], GM[:, j, :, 0:P], lm, ALU.mult).then_inc(sem("nm_out"), 1)

        @block.tensor
        def _(pe):
            mm = nc.tensor.matmul

            def project(i, base_u, m0, rhs, n, width=P, tiles=2, srcs=None):
                for j in range(2):
                    pe.wait_ge(sem(f"w_full{j}"), val(i, 16, 16 * (base_u // 2 + 1)))
                    w = wring[:, j, 0:KT * tiles * width].rearrange("p (k n) -> p k n", k=KT)
                    for t in range(tiles):
                        m = m0 + j * tiles + t
                        pe.wait_ge(sem("p_free"), val(i, 2 * tiles, m + 1))
                        for k in range(KT):
                            last = mm(psum[0:width, m % 2, 0:n], w[:, k, t * width:(t + 1) * width], rhs[:, k, 0:n],
                                      start=(k == 0), stop=(k == KT - 1))
                        last.then_inc(sem("p_done"), 1)

            def sum_squares(o, buf, n):
                for k in range(KT):
                    if k % 4 == 0:
                        pe.wait_ge(sem("n_sq"), 4 * o + k // 4 + 1)
                    last = mm(A[:, 0:n], ones, buf[:, k, 0:n], start=(k == 0), stop=(k == KT - 1))
                last.then_inc(sem("n_ss"), 1)

            def memory(layer):
                o = (0, 3)[layer]
                sum_squares(o, oT, NMEM)
                pe.wait_ge(sem("n_out"), o + 1)
                project(None, U_MEM[layer], M_MEM[layer], oT, NMEM)
                project(None, U_MEM[layer] + 2, M_MEM[layer] + 4, oT, NMEM)
                for h in range(MH):
                    pe.wait_ge(sem("mv_t"), layer * MH + h + 1)
                    pe.wait_ge(sem("mr_out"), layer * MH + h)
                    for t in range(NT):
                        last = nc.tensor.transpose(B[:, t * P:(t + 1) * P], kvp[:, h, t * P:(t + 1) * P], ident)
                    last.then_inc(sem("mr_t"), 1)

            def attend_prompt(h, o, keys, queries, values, causal):
                pe.wait_ge(sem("at_e"), o)
                for t in range(NT):
                    if not causal:
                        last = mm(X[:, t, 0:NMEM], queries[:, t * P:(t + 1) * P], keys, start=True, stop=True)
                        continue
                    for b in range(t + 1):
                        ks = slice(b * P, (b + 1) * P)
                        mm(X[:, t, ks], queries[:, t * P:(t + 1) * P], keys[:, ks], start=True, stop=False)
                        mm(X[:, t, ks], cst[0:FH, C_ONE:C_ONE + P], dm[:, 0, ks], start=False, stop=False)
                        last = mm(X[:, t, ks], dm[:, 1, t * P:(t + 1) * P], cst[0:FH, C_ONE:C_ONE + P], start=False, stop=b < t)
                    last = mm(X[:, t, t * P:(t + 1) * P], ident, cst[:, C_CAUS:C_CAUS + P], start=False, stop=True)
                last.then_inc(sem("at_s"), 1)
                pe.wait_ge(sem("at_p"), o + 1)
                pe.wait_ge(sem("at_pt"), o)
                for t in range(NT):
                    for kt_ in range(NT):
                        if causal and kt_ > t:
                            continue
                        last = nc.tensor.transpose(B[:, kt_ * NPR + t * P:kt_ * NPR + (t + 1) * P],
                                                   Pp[:, t, kt_ * P:(kt_ + 1) * P], ident)
                last.then_inc(sem("at_t"), 1)
                pe.wait_ge(sem("at_pt"), o + 1)
                pe.wait_ge(sem("at_o"), o)
                if causal:
                    mm(Y[:, 0:P], values[:, 0, :], PT[:, 0, 0:P], start=True, stop=True)
                q0 = P if causal else 0
                mm(Y[:, q0:NPR], values[:, 0, :], PT[:, 0, q0:NPR], start=True, stop=False)
                mm(Y[:, q0:NPR], values[:, 1, :], PT[:, 1, q0:NPR], start=False, stop=True).then_inc(sem("at_y"), 1)

            def spread_queries(x, nh, i, per, o):
                pe.wait_ge(sem(x + "_qd"), val(i, per, o + 1))
                for c in range(nh // 4):
                    last = mm((Wp, X[:, 0, :], X[:, 1, :])[c], ones, qd[:, c * 512:(c + 1) * 512], start=True, stop=True)
                last.then_inc(sem(x + "_qb"), 1)

            def softmax_sample(s, x, nh, fox, i, per, o):
                if fox:
                    pe.wait_ge(sem(x + "_ld"), val(i, per, o + 1))
                    n = PAGES * FH
                    mm(A[:, 0:n], cst[:, C_TRI:C_TRI + P], lf[:, bass.ds(s * n, n)], start=True, stop=False)
                    mm(A[:, 0:n], ones, Fs, start=False, stop=False)
                    mm(A[:, 0:n].rearrange("p (g h) -> p g h", h=FH), cst[0:FH, C_ONE:C_ONE + P],
                       ld[0:FH, :].unsqueeze(1).to_broadcast([FH, PAGES, FH]), start=False, stop=True).then_inc(sem(x + "_b"), 1)
                pe.wait_ge(sem(x + "_mx"), val(i, per, o + 1))
                nc.tensor.transpose(B[0:nh, 0:P], mx[:, 0:nh], ident).then_inc(sem(x + "_mt"), 1)
                pe.wait_ge(sem(x + "_dg"), val(i, per, o + 1))
                mm(A[:, 256:256 + nh], cst[0:nh, C_ONE:C_ONE + P], dg[0:nh, 0:nh], start=True, stop=True).then_inc(sem(x + "_mb"), 1)
                pe.wait_ge(sem(x + "_ps"), val(i, per, o + 1))
                mm(A[:, 256:256 + nh], ones, ps[:, 0:nh], start=True, stop=True).then_inc(sem(x + "_den"), 1)

            def weigh_values(nh, ng, fox, full, slots):
                for g in range(ng):
                    full(g)
                    for h in range(nh):
                        last = mm(Y[:, h:h + 1], slots(g, h), Ps[:, g * nh + h:g * nh + h + 1],
                                  start=(g == 0 and h == 0), stop=(g == ng - 1), skip_group_check=True)
                    if fox:
                        last.then_inc(sem("v_used"), 1)
                if not fox:
                    last.then_inc(sem("ms_pv"), 1)

            def memory_samples(layer):
                with pe.Fori(0, NS // 2) as i:
                    for j in range(2):
                        spread_queries("ms", MH, i, 2, layer * NS + j)
                        softmax_sample(None, "ms", MH, False, i, 2, layer * NS + j)
                        weigh_values(MH, 2, False,
                                     lambda g: pe.wait_ge(sem(f"mv_full{j}"), val(i, 16, 16 * (layer * NS // 2 + 1))),
                                     lambda g, h: vring[:, j, g * 512 + h * P:g * 512 + (h + 1) * P])

            pe.wait_ge(sem("const_in"), 16)
            memory(0)
            sum_squares(1, hT, T)
            pe.wait_ge(sem("n_out"), 2)
            with pe.Fori(0, 3) as i:
                project(i, U_Q, M_Q, hT, T)
            project(None, U_QM0, M_QM0, hT, T)
            pe.wait_ge(sem("wf_in"), 16)
            for k in range(KT):
                last = mm(A[0:FH, 0:T], wfb[:, k, :], hT[:, k, :], start=(k == 0), stop=(k == KT - 1))
            last.then_inc(sem("f_y"), 1)
            pe.wait_ge(sem("f_out"), 1)
            for t in range(NT):
                last = nc.tensor.transpose(B[:, t * FH:(t + 1) * FH], fpT[:, t * P:(t + 1) * P], ident[0:FH, 0:FH])
            last.then_inc(sem("f_t"), 1)
            pe.wait_ge(sem("f_row"), 1)
            mm(A[0:FH, 0:P], frow[:, 0, :], cst[:, C_TRI:C_TRI + P], start=True, stop=False)
            mm(A[0:FH, 0:P], frow[:, 1, :], ones, start=False, stop=True)
            mm(A[0:FH, P:2 * P], frow[:, 1, :], cst[:, C_TRI:C_TRI + P], start=True, stop=True).then_inc(sem("d_y"), 1)
            for h in range(MH):
                pe.wait_ge(sem("at_in"), h + 1)
                attend_prompt(h, h, kmT[:, h, :], qh[:, 0, :], vmr[:, :, h, :], False)
            with pe.Fori(0, FH // 2) as i:
                project(i, U_KV, M_KV, hT, T)
                pe.wait_ge(sem("kv_out"), val(i, 1, 1))
                pe.wait_ge(sem("at_pt"), val(i, 2, MH))
                for j in range(2):
                    for t in range(NT):
                        last = nc.tensor.transpose(B[:, (j * NT + t) * P:(j * NT + t + 1) * P],
                                                   kvp[:, 2 + j, t * P:(t + 1) * P], ident)
                last.then_inc(sem("vr_t"), 1)
                pe.wait_ge(sem("vr_out"), val(i, 1, 1))
                for j in range(2):
                    pe.wait_ge(sem("at_in"), val(i, 2, MH + j + 1))
                    o = i * 2 + (MH + j)
                    attend_prompt(None, o, kvp[:, j, 0:NPR], qh[:, j, 0:NPR], vrow[:, j, :, :], True)
            pe.wait_ge(sem("self_p"), 1)
            mm(A[:, 0:FH * NS], ones, prod[:, 0:FH * NS], start=True, stop=True).then_inc(sem("self_y"), 1)
            pe.wait_ge(sem("self_out"), 1)
            def page_values(s):
                weigh_values(FH, PAGES, True,
                             lambda g: pe.wait_ge(sem(f"v_full{g % VRING}"), s * (16 * PAGES // VRING) + 16 * (g // VRING + 1)),
                             lambda g, h: vring[:, g % VRING, h * P:(h + 1) * P])

            spread_queries("fs", FH, None, 1, 0)
            softmax_sample(0, "fs", FH, True, None, 1, 0)
            with pe.Fori(1, NS) as s:
                spread_queries("fs", FH, s, 1, 0)
                page_values(s - 1)
                softmax_sample(s, "fs", FH, True, s, 1, 0)
            page_values(NS - 1)
            memory_samples(0)
            with pe.Fori(0, 4) as i:
                project(i, U_G0, M_G0, hT, T)
            pe.wait_ge(sem("u_out"), 1)
            with pe.Fori(0, 4) as i:
                project(i, U_WO0, M_WO0, gT, T)
            sum_squares(2, hT, T)
            memory(1)
            sum_squares(4, hT, T)
            pe.wait_ge(sem("n_out"), 5)
            project(None, U_LORA, M_LORA, hT, T, width=LORA, tiles=1)
            project(None, U_QM1, M_QM1, hT, T)
            for h in range(MH):
                o = MH + FH + h
                pe.wait_ge(sem("at_in"), o + 1)
                attend_prompt(h, o, kmT[:, h, :], qh[:, 0, :], vmr[:, :, h, :], False)
            memory_samples(1)

            def pair_step(i, j, solve, prepare, fill):
                at = lambda per, k: val(i, 2 * per, per * j + k)
                b, a = j % 2, (j + 1) % 2
                w = runit[:, b, :].rearrange("p (k n) -> p k n", k=KT)

                def project_part(n):
                    if not fill:
                        return
                    t, m = n // 4, M_RKV + 6 + 3 * j + n // 4
                    if n == 0:
                        pe.wait_ge(sem(f"r_full{b}"), val(i, 16, 16 * (j // 2 + 2)))
                    if n % 4 == 0:
                        pe.wait_ge(sem("p_free"), val(i, 6, m + 1))
                    for k in range(4 * (n % 4), 4 * (n % 4) + 4):
                        last = mm(psum[:, m % 2, 0:T], w[:, k, t * P:(t + 1) * P], hT[:, k, :],
                                  start=(k == 0), stop=(k == KT - 1))
                    if n % 4 == 3:
                        last.then_inc(sem("p_done"), 1)

                def lora():
                    if not prepare:
                        return
                    pe.wait_ge(sem(f"v1_full{a}"), val(i, 16, 16 * ((j + 1) // 2 + 1)))
                    pe.wait_ge(sem("prepared"), after(at(1, 1)))
                    mm(A[:, 0:T], vunit[0:LORA, a, 0:P], wlT[0:LORA, 0, :], start=True, stop=True)
                    mm(B[:, 0:T], vunit[0:LORA, a, OFF_A2:OFF_A2 + P], wlT[0:LORA, 1, :], start=True, stop=True)\
                        .then_inc(sem("wa_y"), 1)

                def key_squares():
                    if prepare:
                        pe.wait_ge(sem("wa_out"), at(1, 2))
                        pe.wait_ge(sem("kk_sq"), at(1, 2))
                        mm(A[:, 0:T], blockones, df, start=True, stop=True).then_inc(sem("kk_ss"), 1)

                def bonus_sums():
                    if prepare:
                        pe.wait_ge(sem("rk_p"), at(1, 2))
                        mm(B[:, 0:T], blockones, rn, start=True, stop=True).then_inc(sem("rk_y"), 1)

                def turn(c):
                    if not prepare:
                        return
                    if c == 0:
                        pe.wait_ge(sem("tl_in"), at(1, 2))
                    for n, src in enumerate((bt, kt, sx[:, 2, 0:NPR])):
                        last = nc.tensor.transpose((A, B)[c][:, n * P:(n + 1) * P], src[:, c * P:(c + 1) * P], ident)
                    last.then_inc(sem("rw_t"), 1)

                def products(q):
                    if not prepare:
                        return
                    c, h = q // 2, q % 2
                    hp = slice(64 * h, 64 * h + 64)
                    pe.wait_ge(sem("rw_out"), after(at(2, 4)))
                    if q >= 2:
                        pe.wait_ge(sem("gm_out"), after(at(4, 4 + q - 1)))
                    out = (A, B)[h]
                    mm(out[:, 0:256], bt[hp, c * P:(c + 1) * P], KR[hp, a, c, :], start=True, stop=True)
                    mm(out[:, 256:512], kt[hp, c * P:(c + 1) * P], KR[hp, a, c, :], start=True, stop=True)\
                        .then_inc(sem("gm_y"), 1)

                def sample_sums(n):
                    if not prepare:
                        return
                    pe.wait_ge(sem("gm_out"), after(at(4, 8)))
                    if n == 2:
                        pe.wait_ge(sem("z_used"), at(2, 3))
                    pe.wait_ge(sem("z_in"), at(3, 3 + n + 1))
                    mm((A, B, A)[n], blockones, Z[:, n % 2, :], start=True, stop=True).then_inc(sem("z_y"), 1)

                def level_w(n):
                    if not solve:
                        return
                    pe.wait_ge(sem("nm_out"), at(LEVELS, n + 1))
                    if n == 0:
                        for q in range(4):
                            last = nc.tensor.transpose(Wp[:, q * P:(q + 1) * P], NM[:, 0, q, :], ident)
                    else:
                        pe.wait_ge(sem("tu_out"), at(LEVELS, n))
                        for q in range(4):
                            last = mm(Wp[:, q * P:(q + 1) * P], NM[:, n % 2, q, :], TU[:, q, 0:P], start=True, stop=True)
                    last.then_inc(sem("lv_w"), 1)

                def level_d(n):
                    if not solve:
                        return
                    pe.wait_ge(sem("ws_out"), at(LEVELS - 1, n))
                    for q in range(4):
                        x, at0 = X[:, q // 2, :], (q % 2) * 256
                        mm(x[:, at0:at0 + P], TU[:, q, P:2 * P], Wsb[:, q * P:(q + 1) * P], start=True, stop=True)
                        last = mm(x[:, at0 + P:at0 + 2 * P], Wsb[:, q * P:(q + 1) * P], TU[:, q, P:2 * P], start=True, stop=True)
                    last.then_inc(sem("lv_d"), 1)

                def corrections(c):
                    if not solve:
                        return
                    if c == 0:
                        pe.wait_ge(sem("tu_out"), at(LEVELS, LEVELS))
                    else:
                        pe.wait_ge(sem("st_in"), at(1, 1))
                    for h in range(2):
                        out = Wp[:, h * P:(h + 1) * P]
                        if c:
                            mm(out, KR[:, b, c, 0:P], S0p, start=True, stop=False)
                        last = mm(out, GM[:, b, 2 * c + h, 256:384], rows[:, b, c, 2 * P:3 * P], start=c == 0, stop=True)
                    last.then_inc(sem("c_y"), 1)

                def solved(c):
                    if not solve:
                        return
                    pe.wait_ge(sem("c_out"), at(2, c + 1))
                    for h in range(2):
                        last = mm(Wp[:, (2 + h) * P - 0:(3 + h) * P], TU[:, 2 * c + h, P:2 * P], Cn, start=True, stop=True)
                    last.then_inc(sem("sa_y"), 1)

                def outputs(c):
                    if not solve:
                        return
                    pe.wait_ge(sem("sa_out"), at(2, c + 1))
                    pe.wait_ge(sem("y_out"), after(at(2, c)))
                    v = rows[:, b, c, 2 * P:3 * P]
                    for h in range(2):
                        hp, q = slice(64 * h, 64 * h + 64), 2 * c + h
                        mm(Y[hp, 0:P], SA[:, hp], GM[:, b, q, 128:256], start=True, stop=False)
                        mm(Y[hp, 0:P], v[:, hp], GM[:, b, q, 384:512], start=False, stop=c == 0)
                        if c:
                            mm(Y[hp, 0:P], S0p[:, hp], KR[:, b, c, P:2 * P], start=False, stop=True)
                    mm(Y[:, P:2 * P], rows[:, b, c, 0:P], SA, start=True, stop=False)
                    mm(Y[:, P:2 * P], rows[:, b, c, P:2 * P], v, start=False, stop=True).then_inc(sem("y_y"), 1)

                def group_norm(n):
                    if solve:
                        pe.wait_ge(sem("gn_in"), at(2, n + 1))
                        mm(Y[:, 0:T], blockones, (yT, gdf)[n], start=True, stop=True).then_inc(sem("gn_y"), 1)

                lora()
                level_w(0)
                for n in range(1, LEVELS):
                    level_w(n)
                    if n == 2:
                        key_squares()
                    if n == 3:
                        bonus_sums()
                    project_part(2 * n - 2)
                    if n == 5:
                        turn(0)
                        turn(1)
                    if n == 6:
                        products(0)
                        products(1)
                    level_d(n)
                    project_part(2 * n - 1)
                products(2)
                products(3)
                corrections(0)
                sample_sums(0)
                solved(0)
                sample_sums(1)
                outputs(0)
                corrections(1)
                sample_sums(2)
                solved(1)
                outputs(1)
                group_norm(0)
                group_norm(1)

            pe.wait_ge(sem("lr_out"), 1)
            pair_step(None, -2, False, False, True)
            pair_step(None, -1, False, True, True)
            with pe.Fori(0, RP // 2 - 1) as i:
                for j in range(2):
                    pair_step(i, j, True, True, True)
            pair_step(None, RP - 2, True, True, False)
            pair_step(None, RP - 1, True, False, False)
            with pe.Fori(0, 4) as i:
                project(i, U_G1, M_G1, hT, T)
            pe.wait_ge(sem("u_out"), 2)
            with pe.Fori(0, 4) as i:
                project(i, U_WO1, M_WO1, gT, T)
            sum_squares(5, hT, T)

        @block.scalar
        def _(act):
            ac = nc.scalar.activation
            ch = Chain(act, "act_step")
            act.dma_start(wfb, I["wf"]).then_inc(sem("wf_in"), 16)
            act.sem_inc(sem("p_free"), 2)

            def tile_out(i, per, m, dst, n, func=ACT.Copy, scale=1.0, width=P, then=None):
                act.wait_ge(sem("p_done"), val(i, per, m + 1))
                ac(dst, psum[0:width, m % 2, 0:n], func, scale=scale).then_inc(sem("p_free"), 1)

            def dyn(buf, i, k):
                return buf[:, bass.ds(i + k, 1), :].rearrange("p a t -> p (a t)")

            def root(o, buf):
                act.wait_ge(sem("n_ms"), o + 1)
                ac(buf, buf, ACT.Sqrt).then_inc(sem("n_rt"), 1)

            def memory(layer):
                root((0, 3)[layer], rs[:, 0:NMEM])
                for m in range(8):
                    dst = kmT[:, m, :] if m < 4 else kvp[:, m - 4, 0:NMEM]
                    act.wait_ge(sem("p_done"), M_MEM[layer] + m + 1)
                    if m >= 4:
                        ac(dst, psum[:, m % 2, 0:NMEM], ACT.Copy).then_inc(sem("mv_t"), 1)
                        act.wait_ge(sem("mv_t"), layer * MH + m - 3)
                        act.sem_inc(sem("p_free"), 1)
                    else:
                        ac(dst, psum[:, m % 2, 0:NMEM], ACT.Copy).then_inc(sem("p_free"), 1)
                act.wait_ge(sem("p_free"), M_MEM[layer] + 8 + 2)
                act.dma_start(O["mk"][layer], kmT[:, :, :].rearrange("p h t -> p (h t)")).then_inc(sem("stored_mem"), 16)
                act.dma_start(O["mv"][layer].rearrange("p (h t) -> p h t", h=MH), kvp[:, :, 0:NMEM]).then_inc(sem("stored_mem"), 16)
                for h in range(MH):
                    act.wait_ge(sem("mr_t"), layer * MH + h + 1)
                    ac(vmr[:, :, h, :], B[:, 0:NPR].rearrange("p (t n) -> p t n", t=NT), ACT.Copy).then_inc(sem("mr_out"), 1)
                act.wait_ge(sem("stored_mem"), 32 * (layer + 1))

            def attend_prompt(o, causal, dst):
                act.wait_ge(sem("at_m"), o + 1)
                for t in range(NT):
                    nk = P * (t + 1) if causal else NMEM
                    last = ac(Pp[:, t, 0:nk], X[:, t, 0:nk], ACT.Exp, bias=nm[:, t:t + 1], accum_out=rsum[:, t:t + 1])
                last.then_inc(sem("at_e"), 1)
                act.wait_ge(sem("at_t"), o + 1)
                act.wait_ge(sem("at_y"), o)
                if causal:
                    ac(PT[:, 0, :], B[:, 0:NPR], ACT.Copy)
                    ac(PT[:, 1, P:NPR], B[:, NPR + P:2 * NPR], ACT.Copy).then_inc(sem("at_pt"), 1)
                else:
                    ac(PT[:, :, :].rearrange("p a t -> p (a t)"), B[:, :], ACT.Copy).then_inc(sem("at_pt"), 1)
                act.wait_ge(sem("at_y"), o + 1)
                ac(dst, Y[:, 0:NPR], ACT.Copy).then_inc(sem("at_o"), 1)

            def attend_sample(x, nh, ng, i, per, o):
                act.wait_ge(sem(x + "_qb"), val(i, per, o + 1))
                if x == "ms":
                    act.wait_ge(sem("ms_free"), val(i, per, o + 2))
                else:
                    act.wait_ge(sem("k_used"), val(i, PAGES, PAGES * o))
                for c in range(nh // 4):
                    last = ac(qb[:, c * 512:(c + 1) * 512], (Wp, X[:, 0, :], X[:, 1, :])[c], ACT.Copy)
                last.then_inc(sem(x + "_qbs"), 1)
                act.wait_ge(sem(x + "_sub"), val(i, per, o + 1))
                if x == "fs":
                    ac(pse, pse, ACT.Exp)
                ac(Ps[:, 0:nh * ng], S[:, 0:nh * ng], ACT.Exp).then_inc(sem(x + "_e"), 1)

            def memory_samples(layer):
                with act.Fori(0, NS // 2) as i:
                    for j in range(2):
                        attend_sample("ms", MH, 2, i, 2, layer * NS + j)

            memory(0)
            root(1, rs)
            with act.Fori(0, 3) as i:
                for t in range(4):
                    tile_out(i, 4, M_Q + t, dyn(qT, i * 4, t), T, scale=SCALE)
            for t in range(4):
                tile_out(None, 4, M_QM0 + t, qT[:, FH + t, :], T, scale=SCALE)
            act.wait_ge(sem("f_abs"), 1)
            ch.do(ac(ftmp, ftmp, ACT.Exp, scale=-1.0))
            ac(ftmp, ftmp, ACT.Ln, bias=1.0).then_inc(sem("f_ln"), 1)
            act.wait_ge(sem("f_out"), 1)
            act.dma_start(O["lf"], fpT).then_inc(sem("stored_lf"), 16)
            act.wait_ge(sem("f_t"), 1)
            ac(frow.rearrange("p t h -> p (t h)"), B[:, 0:NT * FH], ACT.Copy).then_inc(sem("f_row"), 1)
            act.wait_ge(sem("d_y"), 1)
            ac(dT, A[0:FH, 0:NPR], ACT.Copy).then_inc(sem("d_out"), 1)
            for h in range(MH):
                attend_prompt(h, False, oT[:, FH + h, 0:NPR])
            with act.Fori(0, FH // 2) as i:
                act.wait_ge(sem("stored_kv"), after(val(i, 32, 0)))
                act.wait_ge(sem("kv_free"), after(val(i, 1, 0)))
                for t in range(4):
                    act.wait_ge(sem("p_done"), val(i, 4, M_KV + t + 1))
                    ac(kvp[:, t, :], psum[:, t % 2, 0:T], ACT.Copy)
                    ac((kS, vS)[t // 2][:, bass.ds(i * 2 + t % 2, 1), :].rearrange("p a t -> p (a t)"),
                       psum[:, t % 2, NPR:T], ACT.Copy).then_inc(sem("p_free"), 1)
                act.wait_ge(sem("p_free"), val(i, 4, M_KV + 4 + 2))
                act.sem_inc(sem("kv_out"), 1)
                for n, name in enumerate(("fk", "fv")):
                    act.dma_start(O[name][:, bass.ds(i * (2 * T), 2 * T)],
                                  kvp[:, 2 * n:2 * n + 2, :].rearrange("p a t -> p (a t)")).then_inc(sem("stored_kv"), 16)
                act.wait_ge(sem("vr_t"), val(i, 1, 1))
                act.wait_ge(sem("at_y"), val(i, 2, MH))
                ac(vrow, B.rearrange("p (h t n) -> p h t n", h=2, t=NT), ACT.Copy).then_inc(sem("vr_out"), 1)
                for j in range(2):
                    attend_prompt(i * 2 + (MH + j), True, oT[:, bass.ds(i * 2 + j, 1), 0:NPR].rearrange("p a t -> p (a t)"))
            attend_sample("fs", FH, PAGES, None, 1, 0)
            with act.Fori(1, NS) as s:
                attend_sample("fs", FH, PAGES, s, 1, 0)
            memory_samples(0)
            with act.Fori(0, 4) as i:
                for t in range(4):
                    tile_out(i, 4, M_G0 + t, dyn(gT, i * 4, t), T, func=ACT.Silu)
            act.wait_ge(sem("u_out"), 1)
            with act.Fori(0, 4) as i:
                for t in range(4):
                    tile_out(i, 4, M_WO0 + t, dyn(oT, i * 4, t), T)
            root(2, rs)
            act.wait_ge(sem("stored_kv"), after(32 * FH // 2))
            memory(1)
            root(4, rs)
            act.wait_ge(sem("lr_free"), 1)
            for t in range(2):
                tile_out(None, 2, M_LORA + t, pb[0:LORA, 0, t, 1:T + 1], T, width=LORA)
            act.wait_ge(sem("lr_s"), 1)
            ac(wlT[0:LORA, 0, :], sx[0:LORA, 0, :], ACT.Tanh)
            ac(wlT[0:LORA, 1, :], sx[0:LORA, 1, :], ACT.Copy).then_inc(sem("lr_out"), 1)
            for t in range(4):
                tile_out(None, 4, M_QM1 + t, qT1[:, t, :], T, scale=SCALE)
            for h in range(MH):
                attend_prompt(MH + FH + h, False, oT[:, FH + h, 0:NPR])
            memory_samples(1)
            def pair_step(i, j, solve, prepare, fill):
                at = lambda per, k: val(i, 2 * per, per * j + k)
                b, a = j % 2, (j + 1) % 2
                vec = lambda n: vunit[:, a, OFF_V + n:OFF_V + n + 1]

                def projected(t):
                    if fill:
                        if t == 0 and j != -2:
                            act.wait_ge(sem("mix"), after(at(1, 1)))
                        tile_out(i, 6, M_RKV + 6 + 3 * j + t, pb[:, b, t, 1:T + 1], T)

                def level(n):
                    if solve:
                        act.wait_ge(sem("lv_w"), after(at(LEVELS, n + 1)))
                        ac(Wsb, Wp, ACT.Copy).then_inc(sem("ws_out"), 1)

                def chain(c):
                    if solve:
                        own = lambda x: x.rearrange("p (h x) -> p h x", h=2)[:, :, 0:64]
                        two = lambda x: x.rearrange("p (h x) -> p h x", h=2)
                        act.wait_ge(sem("c_y"), at(2, c + 1))
                        ac(two(Cn), own(Wp[:, 0:384]), ACT.Copy, scale=-1.0).then_inc(sem("c_out"), 1)
                        act.wait_ge(sem("sa_y"), at(2, c + 1))
                        ac(SA[:, 0:64], Wp[:, 256:320], ACT.Copy)
                        ac(SA[:, 64:P], Wp[:, 448:512], ACT.Copy).then_inc(sem("sa_out"), 1)

                if prepare:
                    act.wait_ge(sem("wa_y"), at(1, 2))
                    ac(lw, A[:, 0:T], ACT.Sigmoid, bias=vec(W0))
                    ac(aa, B[:, 0:T], ACT.Sigmoid, bias=vec(A0)).then_inc(sem("wa_out"), 1)
                level(1)
                level(2)
                if prepare:
                    act.wait_ge(sem("kk_ss"), at(1, 2))
                    ac(kk, A[:, 0:T], ACT.Sqrt).then_inc(sem("kk_rt"), 1)
                projected(0)
                level(3)
                if prepare:
                    act.wait_ge(sem("cum"), at(1, 2))
                    ac(E1, cc[:, 0:NPR], ACT.Exp)
                    ac(E2, cc[:, 0:NPR], ACT.Exp, scale=-1.0)
                    ac(sc4[:, a, :], sc4[:, a, :], ACT.Exp)
                    ac(E3, E3, ACT.Exp)
                    ac(lw[:, NPR:T], lw[:, NPR:T], ACT.Exp).then_inc(sem("ex_out"), 1)
                level(4)
                projected(1)
                level(5)
                if prepare:
                    for c in range(NT):
                        act.wait_ge(sem("rw_t"), at(2, 2 + c + 1))
                        ac(rows[:, a, c, :], (A, B)[c][:, 0:3 * P], ACT.Copy).then_inc(sem("rw_out"), 1)
                level(6)
                projected(2)
                for c in range(NT):
                    chain(c)
                if prepare:
                    act.wait_ge(sem("ss_out"), at(1, 2))
                    act.dma_start(O["ws"][bass.ds(i * 2 + (j + 1), 1)].rearrange("a p n -> (a p) n") if i is not None else O["ws"][j + 1],
                                  s0[:, a, :]).then_inc(sem(f"pair_stored{a}"), 16)
                if solve:
                    act.wait_ge(sem("gn_ms"), at(1, 1))
                    ac(grn, grn, ACT.Sqrt).then_inc(sem("gn_rt"), 1)
                    act.wait_ge(sem("st_out"), at(1, 1))
                    act.dma_start(O["wp"][bass.ds(i * 2 + j, 1)].rearrange("a p n -> (a p) n") if i is not None else O["wp"][j],
                                  ST).then_inc(sem("pair_stored_p"), 16)

            pair_step(None, -2, False, False, True)
            pair_step(None, -1, False, True, True)
            with act.Fori(0, RP // 2 - 1) as i:
                for j in range(2):
                    pair_step(i, j, True, True, True)
            pair_step(None, RP - 2, True, True, False)
            pair_step(None, RP - 1, True, False, False)
            act.wait_ge(sem("mix"), after(RP))
            act.dma_start(O["sh"], shout[:, :, :].rearrange("p a b -> p (a b)")).then_inc(sem("stored_sh"), 16)
            act.wait_ge(sem("pair_done"), after(RP))
            with act.Fori(0, 4) as i:
                for t in range(4):
                    tile_out(i, 4, M_G1 + t, dyn(gT, i * 4, t), T, func=ACT.Silu)
            act.wait_ge(sem("u_out"), 2)
            with act.Fori(0, 4) as i:
                for t in range(4):
                    tile_out(i, 4, M_WO1 + t, dyn(oT, i * 4, t), T)
            root(5, rs)
            act.wait_ge(sem("x_out"), 2)
            act.dma_start(O["yT"], xT[:, :, :].rearrange("p k t -> p (k t)")).then_inc(sem("stored_y"), 16)
            act.wait_ge(sem("stored_y"), 16)
            act.wait_ge(sem("stored_lf"), 16)
            act.wait_ge(sem("stored_sh"), 16)
            act.wait_ge(sem("stored_kv"), after(32 * FH // 2))
            for j in range(2):
                act.wait_ge(sem(f"pair_stored{j}"), 16 * RP // 2)
            act.wait_ge(sem("pair_stored_p"), after(16 * RP))

        @block.vector
        def _(dve):
            v_ = nc.vector
            tt, ts, stt = v_.tensor_tensor, v_.tensor_scalar, v_.scalar_tensor_tensor
            ch = Chain(dve, "dve_step")

            def squares(o, dst, src, n):
                for c in range(4):
                    tt(dst[:, 4 * c:4 * c + 4, 0:n], src[:, 4 * c:4 * c + 4, 0:n], src[:, 4 * c:4 * c + 4, 0:n],
                       ALU.mult).then_inc(sem("n_sq"), 1)

            def inverse_root(o, n):
                dve.wait_ge(sem("n_ss"), o + 1)
                ts(rs[:, 0:n], A[:, 0:n], 1.0 / D, RMS_EPS, ALU.mult, ALU.add).then_inc(sem("n_ms"), 1)
                dve.wait_ge(sem("n_rt"), o + 1)
                ch.do(v_.reciprocal(rs[:, 0:n], rs[:, 0:n]))

            def norm(o, dst, src, n, g):
                squares(o, dst, src, n)
                inverse_root(o, n)
                for k in range(KT):
                    last = stt(dst[:, k, 0:n], src[:, k, 0:n], g[:, k:k + 1], rs[:, 0:n], ALU.mult, ALU.mult)
                last.then_inc(sem("n_out"), 1)

            memv = gflat[:, 0:KT * NMEM].rearrange("p (k t) -> p k t", k=KT)

            def attend_prompt(o, causal):
                dve.wait_ge(sem("at_s"), o + 1)
                for t in range(NT):
                    nk = P * (t + 1) if causal else NMEM
                    last = v_.tensor_reduce(nm[:, t:t + 1], X[:, t, 0:nk], AX.X, ALU.max, negate=True)
                last.then_inc(sem("at_m"), 1)
                dve.wait_ge(sem("at_e"), o + 1)
                ch.do(v_.reciprocal(rinv, rsum))
                for t in range(NT):
                    nk = P * (t + 1) if causal else NMEM
                    last = ts(Pp[:, t, 0:nk], Pp[:, t, 0:nk], rinv[:, t:t + 1], None, ALU.mult)
                last.then_inc(sem("at_p"), 1)

            def memory_prompt(base, q):
                for h in range(MH):
                    dve.wait_ge(sem("at_s"), base + h)
                    v_.tensor_copy(qh[:, 0, 0:NPR], q[:, h, 0:NPR]).then_inc(sem("at_in"), 1)
                    attend_prompt(base + h, False)

            def score(x, nh, ng, q, full, page, i, per, o):
                fox = x == "fs"
                tt(qd[:, 0:nh * P].rearrange("p (h n) -> p h n", h=nh), ident.unsqueeze(1).to_broadcast([P, nh, P]),
                   q.to_broadcast([P, nh, P]), ALU.mult).then_inc(sem(x + "_qd"), 1)
                dve.wait_ge(sem(x + "_qbs"), val(i, per, o + 1))
                for g in range(ng):
                    full(g)
                    for h in range(nh):
                        last = v_.tensor_tensor_reduce(page(g, h), page(g, h), qb[:, h * P:(h + 1) * P], 1.0, 0.0,
                                                       ALU.mult, ALU.add, S[:, g * nh + h:g * nh + h + 1])
                    if fox:
                        last.then_inc(sem("k_used"), 1)
                    elif g == ng - 1:
                        last.then_inc(sem("ms_kd"), 1)

            def softmax(x, s, nh, ng, i, per, o):
                g3 = lambda b: b[:, 0:ng * nh].rearrange("p (g h) -> p g h", h=nh)
                bc = lambda b: b[:, 0:nh].unsqueeze(1).to_broadcast([P, ng, nh])
                fox = x == "fs"
                if fox:
                    lfs = lambda g: lf[:, bass.ds(s * (PAGES * FH) + g * FH, FH)]
                    ch.do(v_.memset(Fs[:, (PAGES - 1) * FH:PAGES * FH], 0.0))
                    for g in range(PAGES - 2, -1, -1):
                        ch.do(tt(Fs[:, g * FH:(g + 1) * FH], Fs[:, (g + 1) * FH:(g + 2) * FH], lfs(g + 1), ALU.add))
                    ts(ld[0:FH, :], ident[0:FH, 0:FH], fpT[:, bass.ds(s + NPR, 1)], None, ALU.mult).then_inc(sem(x + "_ld"), 1)
                    dve.wait_ge(sem(x + "_b"), val(i, per, o + 1))
                    dve.wait_ge(sem("k_used"), s * PAGES + PAGES)
                    ch.do(tt(S, S, A[:, 0:ng * nh], ALU.add))
                else:
                    dve.wait_ge(sem("ms_kd"), val(i, per, o + 1))
                v_.tensor_reduce(mx[:, 0:nh], S[:, 0:ng * nh].rearrange("p (g h) -> p h g", h=nh), AX.X, ALU.max)\
                    .then_inc(sem(x + "_mx"), 1)
                dve.wait_ge(sem(x + "_mt"), val(i, per, o + 1))
                ch.do(v_.tensor_reduce(m12[0:nh, :], B[0:nh, 0:P], AX.X, ALU.max))
                ts(dg[0:nh, 0:nh], ident[0:nh, 0:nh], m12[0:nh, 0:1], None, ALU.mult).then_inc(sem(x + "_dg"), 1)
                dve.wait_ge(sem(x + "_mb"), val(i, per, o + 1))
                if fox:
                    me = selfS[:, :, bass.ds(s, 1)].rearrange("p h a -> p (h a)")
                    ch.do(tt(mb[:, 0:nh], A[:, 256:256 + nh], me, ALU.max))
                    tt(pse, me, mb, ALU.subtract)
                else:
                    ch.do(v_.tensor_copy(mb[:, 0:nh], A[:, 256:256 + nh]))
                if fox:
                    dve.wait_ge(sem(x + "_dg"), val(i, per, o + 1))
                tt(g3(S), g3(S), bc(mb), ALU.subtract).then_inc(sem(x + "_sub"), 1)
                dve.wait_ge(sem(x + "_e"), val(i, per, o + 1))
                v_.tensor_reduce(ps[:, 0:nh], Ps[:, 0:ng * nh].rearrange("p (g h) -> p h g", h=nh), AX.X, ALU.add)\
                    .then_inc(sem(x + "_ps"), 1)
                dve.wait_ge(sem(x + "_den"), val(i, per, o + 1))
                if fox:
                    ch.do(tt(rden[:, 0:nh], A[:, 256:256 + nh], pse[:, 0:nh], ALU.add))
                    ch.do(v_.reciprocal(rden[:, 0:nh], rden[:, 0:nh]))
                    ch.do(tt(osum, vS[:, :, bass.ds(s, 1)].rearrange("p h a -> p (h a)"), pse, ALU.mult))
                else:
                    ch.do(v_.reciprocal(rden[:, 0:nh], A[:, 256:256 + nh]))

            def finish(x, s, nh, out, i, per, o):
                if x == "fs":
                    dve.wait_ge(sem("v_used"), s * PAGES + PAGES)
                    ch.do(tt(osum, osum, Y[:, 0:nh], ALU.add))
                    ch.do(tt(out, osum[:, 0:nh].unsqueeze(2), rden[:, 0:nh].unsqueeze(2), ALU.mult))
                else:
                    dve.wait_ge(sem("ms_pv"), val(i, per, o + 1))
                    tt(out, Y[:, 0:nh].unsqueeze(2), rden[:, 0:nh].unsqueeze(2), ALU.mult).then_inc(sem("ms_free"), 1)

            def memory_samples(layer, q):
                with dve.Fori(0, NS // 2) as i:
                    ch.enter(i, 2 * 3)
                    for j in range(2):
                        s = i * 2 + (NPR + j)
                        score("ms", MH, 2, q[:, :, bass.ds(s, 1)],
                              lambda g: dve.wait_ge(sem(f"mk_full{j}"), val(i, 16, 16 * (layer * NS // 2 + 1))),
                              lambda g, h: kring[:, j, g * 512 + h * P:g * 512 + (h + 1) * P], i, 2, layer * NS + j)
                        softmax("ms", None, MH, 2, i, 2, layer * NS + j)
                        finish("ms", None, MH, oT[:, FH:KT, bass.ds(s, 1)], i, 2, layer * NS + j)
                    ch.leave(NS // 2)

            def gated(n, samples):
                dve.wait_ge(sem("ms_free"), samples + 2)
                dve.wait_ge(sem("p_free"), n)
                for c in range(4):
                    last = tt(gT[:, 4 * c:4 * c + 4, :], oT[:, 4 * c:4 * c + 4, :], gT[:, 4 * c:4 * c + 4, :], ALU.mult)
                last.then_inc(sem("u_out"), 1)

            def residual(o, n, layer):
                dve.wait_ge(sem("p_free"), n)
                squares(o, hT, oT, T)
                inverse_root(o, T)
                g = gpost(layer)
                for k in range(KT):
                    last = stt(oT[:, k, :], oT[:, k, :], g[:, k:k + 1], rs, ALU.mult, ALU.mult)
                ch.do(last)
                for c in range(4):
                    last = tt(xT[:, 4 * c:4 * c + 4, :], xT[:, 4 * c:4 * c + 4, :], oT[:, 4 * c:4 * c + 4, :], ALU.add)
                ch.do(last)
                dve.sem_inc(sem("n_out"), 1)
                dve.sem_inc(sem("x_out"), 1)

            for name in ahead:
                dve.sem_inc(sem(name), 1)
            dve.sem_inc(sem("ms_free"), 2)
            dve.wait_ge(sem("const_in"), 16)
            dve.wait_ge(sem("vec_in"), 16)
            dve.wait_ge(sem("mem_in0"), 16)
            norm(0, oT, memv, NMEM, gmem(0))
            dve.wait_ge(sem("x_in"), 16)
            norm(1, hT, xT, T, gpre(0))
            dve.wait_ge(sem("vec_in2"), 16)
            dve.wait_ge(sem("f_y"), 1)
            ch.do(ts(fpT, A[0:FH, 0:T], bf[:, 0:1], None, ALU.add))
            ch.do(ts(ftmp, fpT, -1.0, None, ALU.mult))
            tt(ftmp, ftmp, fpT, ALU.max).then_inc(sem("f_abs"), 1)
            ch.do(ts(fpT, fpT, 0.0, None, ALU.min))
            dve.wait_ge(sem("f_ln"), 1)
            tt(fpT, fpT, ftmp, ALU.subtract).then_inc(sem("f_out"), 1)
            dve.wait_ge(sem("p_free"), M_QM0 + 4 + 2)
            dve.wait_ge(sem("mr_out"), MH)
            memory_prompt(0, qT[:, FH:KT, :])
            dve.wait_ge(sem("d_out"), 1)
            dve.wait_ge(sem("f_out"), 1)
            with dve.Fori(0, FH // 2) as i:
                ch.enter(i, 2)
                dve.wait_ge(sem("at_s"), val(i, 2, MH))
                v_.tensor_copy(qh[:, :, 0:NPR], qT[:, bass.ds(i * 2, 2), 0:NPR])
                for j in range(2):
                    dve.wait_ge(sem("at_s"), val(i, 2, MH + j))
                    sel = ident[0:FH, bass.ds(i * 2 + j, 1)]
                    ts(dm[:, 0, :], dT, sel, None, ALU.mult)
                    ts(dm[:, 1, :], dT, sel, -1.0, ALU.mult, ALU.mult).then_inc(sem("at_in"), 1)
                    attend_prompt(i * 2 + (MH + j), True)
                dve.wait_ge(sem("at_s"), val(i, 2, MH + 2))
                dve.wait_ge(sem("at_in"), val(i, 2, MH + 2))
                dve.sem_inc(sem("kv_free"), 1)
                ch.leave(FH // 2)
            dve.wait_ge(sem("p_free"), M_KV + 24 + 2)
            dve.wait_ge(sem("at_o"), MH + FH)
            tt(prod[:, 0:FH * NS].rearrange("p (h s) -> p h s", h=FH), qT[:, 0:FH, NPR:T], kS, ALU.mult).then_inc(sem("self_p"), 1)
            dve.wait_ge(sem("self_y"), 1)
            v_.tensor_copy(selfS.rearrange("p h s -> p (h s)"), A[:, 0:FH * NS]).then_inc(sem("self_out"), 1)
            dve.wait_ge(sem("self_out"), 1)
            def column(buf, s):
                return buf[:, 0:FH, NPR + s:NPR + s + 1] if isinstance(s, int) else buf[:, 0:FH, bass.ds(s + NPR, 1)]

            def pages(s, i):
                score("fs", FH, PAGES, column(qT, s),
                      lambda g: dve.wait_ge(sem(f"k_full{g % KRING}"), s * (32 * PAGES // KRING) + 32 * (g // KRING + 1)),
                      lambda g, h: kring[:, g % KRING, h * P:(h + 1) * P], i, 1, 0)

            pages(0, None)
            softmax("fs", 0, FH, PAGES, None, 1, 0)
            with dve.Fori(1, NS) as s:
                ch.enter(s - 1, 24)
                pages(s, s)
                finish("fs", s - 1, FH, column(oT, s - 1), s, 1, 0)
                softmax("fs", s, FH, PAGES, s, 1, 0)
                ch.leave(NS - 1)
            finish("fs", NS - 1, FH, column(oT, NS - 1), None, 1, 0)
            memory_samples(0, qT[:, FH:KT, :])
            gated(M_G0 + 16 + 2, NS)
            residual(2, M_WO0 + 16 + 2, 0)
            dve.wait_ge(sem("mem_in1"), 16)
            norm(3, oT, memv, NMEM, gmem(1))
            norm(4, hT, xT, T, gpre(1))
            for n in range(3, 5):
                dve.wait_ge(sem(f"vec_in{n}"), 16)
            ch.do(v_.memset(pb[:, :, :, 0:1], 0.0))
            dve.sem_inc(sem("lr_free"), 1)

            def shift(x, rows_, p_, prev, mu, dst):
                p_ = p_[0:rows_, :]
                cur = p_[:, 1:T + 1]
                tt(df[0:rows_, 0:NPR], p_[:, 0:NPR], cur[:, 0:NPR], ALU.subtract)
                ch.do(tt(df[0:rows_, NPR:T], prev, cur[:, NPR:T], ALU.subtract))
                ch.do(stt(sx[0:rows_, x, :], df[0:rows_, :], mu, cur, ALU.mult, ALU.add))
                return v_.tensor_copy(dst, p_[:, NPR:T + 1])

            dve.wait_ge(sem("p_free"), M_LORA + 2 + 2)
            v_.memset(shout[:, SHT - 2:SHT, :], 0.0)
            for x in range(2):
                last = shift(x, LORA, pb[:, 0, x, :], shL[0:LORA, x, :], muL[0:LORA, x:x + 1], shout[0:LORA, SHT - 2 + x, :])
            last.then_inc(sem("lr_s"), 1)
            dve.wait_ge(sem("lr_out"), 1)
            dve.wait_ge(sem("p_free"), M_QM1 + 4 + 2)
            dve.wait_ge(sem("mr_out"), 2 * MH)
            memory_prompt(MH + FH, qT1)
            dve.wait_ge(sem("at_o"), 2 * MH + FH)
            memory_samples(1, qT1)
            dve.wait_ge(sem("vec_in5"), 16)

            def pair_step(i, j, solve, prepare):
                at = lambda per, k: val(i, 2 * per, per * j + k)
                b, a = j % 2, (j + 1) % 2
                o = i * 2 + j if i is not None else j
                col = lambda n: vunit[:, a, OFF_V + n:OFF_V + n + 1]
                r, k, v = (sx[:, x, :] for x in range(3))
                bo = bonus[:, a, :]
                c3 = lambda x: x.rearrange("p (c t) -> p c t", c=NT)
                x3 = lambda x: x.rearrange("p (s v) -> p s v", s=NS)
                bs = lambda x: x[:, NPR:T].unsqueeze(2).to_broadcast([P, NS, 64])
                i64 = cst[:, C_I64:C_I64 + 64].unsqueeze(1).to_broadcast([P, NS, 64])
                s3 = x3(s0[:, a, :])

                def first():
                    if not solve:
                        return
                    idb = ident.unsqueeze(1).to_broadcast([P, 4, P])
                    dve.wait_ge(sem("nm_out"), at(LEVELS, 1))
                    tt(TU[:, :, P:2 * P], idb, NM[:, 0, :, :], ALU.subtract)
                    dve.wait_ge(sem("lv_w"), after(at(LEVELS, 1)))
                    tt(TU[:, :, 0:P], idb, Wp.rearrange("p (q t) -> p q t", q=4), ALU.subtract).then_inc(sem("tu_out"), 1)

                def level(n):
                    if solve:
                        dve.wait_ge(sem("lv_d"), at(LEVELS - 1, n))
                        tt(TU, TU, X.rearrange("p b (q n) -> p (b q) n", q=2), ALU.subtract).then_inc(sem("tu_out"), 1)

                def mix():
                    for name in ("v1_full", "s0_full"):
                        dve.wait_ge(sem(f"{name}{a}"), val(i, 16, 16 * ((j + 1) // 2 + 1)))
                    dve.wait_ge(sem("p_free"), val(i, 6, M_RKV + 3 * j + 6 + 2))
                    for x in range(3):
                        dst = shout[:, bass.ds((o + 1) * 3 + x, 1), :].rearrange("p a t -> p (a t)") if i is not None \
                            else shout[:, (o + 1) * 3 + x, :]
                        last = shift(x, P, pb[:, a, x, :], vunit[:, a, OFF_SH + x * NS:OFF_SH + (x + 1) * NS], col(MU_R + x), dst)
                    last.then_inc(sem("mix"), 1)

                def keys():
                    dve.wait_ge(sem("mix"), after(at(1, 2)))
                    ch.do(ts(kkr, k, col(K_K), None, ALU.mult))
                    tt(df, kkr, kkr, ALU.mult).then_inc(sem("kk_sq"), 1)
                    dve.wait_ge(sem("wa_out"), at(1, 2))
                    ch.do(ts(km, aa, 1.0, col(K_A), ALU.subtract, ALU.mult))
                    ch.do(stt(km, km, 1.0, k, ALU.add, ALU.mult))
                    stt(rn, r, col(R_K), km, ALU.mult, ALU.mult).then_inc(sem("rk_p"), 1)

                def decays():
                    ch.do(ts(lw, lw, -EXPM, None, ALU.mult))
                    for c in range(4):
                        last = v_.tensor_tensor_scan(cc[:, c * 64:c * 64 + 64], cst[:, C_ONE:C_ONE + 64], lw[:, c * 64:c * 64 + 64],
                                                     0.0, ALU.mult, ALU.add)
                    ch.do(last)
                    ends = cc[:, 0:NPR].rearrange("p (a t) -> p a t", a=4)[:, :, 63]
                    v_.tensor_copy(sc4[:, a, :], ends)
                    ch.do(v_.tensor_copy(hs4, ends))
                    for c in range(NT):
                        last = ts(cc[:, c * P:c * P + 64], cc[:, c * P:c * P + 64], hs4[:, 2 * c:2 * c + 1], None, ALU.subtract)
                    ch.do(last)
                    tt(E3, cc[:, 0:NPR], lw[:, 0:NPR], ALU.subtract).then_inc(sem("cum"), 1)

                def normal_keys():
                    dve.wait_ge(sem("kk_rt"), at(1, 2))
                    ch.do(ts(kk, kk, 1e-12, None, ALU.max))
                    ch.do(v_.reciprocal(kk, kk))
                    ch.do(tt(kk, kkr, kk, ALU.mult))
                    dve.wait_ge(sem("rk_y"), at(1, 2))
                    ch.do(tt(bo, B[:, 0:T], v, ALU.mult))
                    ch.do(tt(bb, kk, aa, ALU.mult))

                def scaled():
                    dve.wait_ge(sem("ex_out"), at(1, 2))
                    tt(KR[:, a, :, 0:P], c3(kk[:, 0:NPR]), c3(E3), ALU.mult)
                    tt(KR[:, a, :, P:2 * P], c3(r[:, 0:NPR]), c3(E1), ALU.mult)
                    tt(bt, bb[:, 0:NPR], E2, ALU.mult)
                    tt(kt, km[:, 0:NPR], E2, ALU.mult).then_inc(sem("tl_in"), 1)

                def matrix(q):
                    dve.wait_ge(sem("gm_y"), at(4, 4 + q + 1))
                    tt(GM[:, a, q, :], (A, B)[q % 2], masks[:, K_RM:K_RM + 512], ALU.mult).then_inc(sem("gm_out"), 1)

                first()
                if prepare:
                    mix()
                level(1)
                if prepare:
                    keys()
                level(2)
                if prepare:
                    decays()
                level(3)
                if prepare:
                    normal_keys()
                level(4)
                if prepare:
                    scaled()
                level(5)
                if prepare:
                    matrix(0)
                    matrix(1)
                level(6)
                if prepare:
                    matrix(2)
                    matrix(3)
                    tt(x3(Z[:, 0, :]), s3, bs(kk), ALU.mult).then_inc(sem("z_in"), 1)
                    tt(x3(Z[:, 1, :]), i64, bs(v), ALU.mult).then_inc(sem("z_in"), 1)
                    ch.do(tt(s3, s3, bs(lw), ALU.mult))
                if solve:
                    dve.wait_ge(sem("y_y"), at(2, 1))
                    v_.tensor_copy(yT[:, 0:P], Y[:, 0:P])
                    dve.wait_ge(sem("pair_stored_p"), after(at(16, 0)))
                    ch.do(stt(ST, Y[:, P:2 * P], sc4[:, b, 1:2], blockones, ALU.mult, ALU.mult))
                    ch.do(ts(S0p, ST, sc4[:, b, 2:3], None, ALU.mult))
                    dve.sem_inc(sem("st_in"), 1)
                    dve.sem_inc(sem("y_out"), 1)
                if prepare:
                    zt = x3(Z[:, 0, :])
                    dve.wait_ge(sem("z_y"), at(3, 3 + 1))
                    ch.do(tt(zt, x3(A), bs(bb), ALU.mult))
                    dve.sem_inc(sem("z_used"), 1)
                    ch.do(tt(s3, s3, zt, ALU.subtract))
                    dve.wait_ge(sem("z_y"), at(3, 3 + 2))
                    ch.do(tt(zt, x3(B), bs(km), ALU.mult))
                    dve.sem_inc(sem("z_used"), 1)
                    tt(s3, s3, zt, ALU.add).then_inc(sem("ss_out"), 1)
                    dve.wait_ge(sem("ss_out"), at(1, 2))
                    tt(zt, s3, bs(r), ALU.mult).then_inc(sem("z_in"), 1)
                if solve:
                    dve.wait_ge(sem("y_y"), at(2, 2))
                    v_.tensor_copy(yT[:, P:2 * P], Y[:, 0:P])
                    v_.tensor_copy(yT[:, NPR:T], ys[:, b, :])
                    ch.do(tt(ST, S0p, Y[:, P:2 * P], ALU.add))
                    ch.do(stt(ST, ST, sc4[:, b, 3:4], blockones, ALU.mult, ALU.mult))
                    dve.sem_inc(sem("st_out"), 1)
                    dve.sem_inc(sem("y_out"), 1)
                    dve.sem_inc(sem("gn_in"), 1)
                if prepare:
                    dve.wait_ge(sem("z_y"), at(3, 3 + 3))
                    ch.do(tt(x3(Z[:, 1, :]), x3(A), i64, ALU.mult))
                    ch.do(v_.tensor_reduce(ys[:, a, :], x3(Z[:, 1, :]), AX.X, ALU.add))
                    dve.sem_inc(sem("prepared"), 1)
                if solve:
                    dve.wait_ge(sem("gn_y"), at(2, 1))
                    ch.do(stt(yT, Y[:, 0:T], -1.0 / 64, yT, ALU.mult, ALU.add))
                    ch.do(tt(gdf, yT, yT, ALU.mult))
                    dve.sem_inc(sem("gn_in"), 1)
                    dve.wait_ge(sem("gn_y"), at(2, 2))
                    ch.do(ts(grn, Y[:, 0:T], 1.0 / 64, GN_EPS, ALU.mult, ALU.add))
                    dve.sem_inc(sem("gn_ms"), 1)
                    dve.wait_ge(sem("gn_rt"), at(1, 1))
                    ch.do(v_.reciprocal(grn, grn))
                    ln = lambda n: lnv[:, bass.ds(o, 1), n:n + 1].rearrange("p a b -> p (a b)") if i is not None else lnv[:, o, n:n + 1]
                    ch.do(stt(yT, yT, ln(0), grn, ALU.mult, ALU.mult))
                    out = oT[:, bass.ds(o, 1), :].rearrange("p a t -> p (a t)") if i is not None else oT[:, o, :]
                    ch.do(stt(out, yT, ln(1), bonus[:, b, :], ALU.add, ALU.add))
                    dve.sem_inc(sem("pair_done"), 1)

            ch.do(v_.memset(pb[:, :, :, 0:1], 0.0))
            dve.wait_ge(sem("masks_in"), 16)
            pair_step(None, -1, False, True)
            with dve.Fori(0, RP // 2 - 1) as i:
                ch.enter(i, STEPS)
                for j in range(2):
                    pair_step(i, j, True, True)
                ch.leave(RP // 2 - 1)
            pair_step(None, RP - 2, True, True)
            pair_step(None, RP - 1, True, False)
            gated(M_G1 + 16 + 2, 2 * NS)
            residual(5, M_WO1 + 16 + 2, 1)


_OUTS = {"yT": (P, KT * T), "mk": (2, P, MH * NMEM), "mv": (2, P, MH * NMEM), "fk": (P, FH * T), "fv": (P, FH * T),
         "lf": (FH, T), "sh": (P, SHT * 9), "wp": (RP, P, P), "ws": (RP, P, NS * 64)}


def kernel(**inputs):
    import concourse.bacc as bacc
    from concourse.bass_utils import run_bass_kernel_spmd as run

    x = {k: np.asarray(v) for k, v in inputs.items()}

    def tiles(a):
        return a.reshape(-1, P, a.shape[1]).transpose(1, 0, 2)

    def units(w, cols=U):
        n = w.shape[1] // cols
        return w.reshape(KT, P, n, cols).transpose(2, 1, 0, 3).reshape(n, P, KT * cols)

    def columns(a):
        return a.reshape(-1, P).T

    A_ = {}
    A_["consts"], A_["masks"] = shape_constants()
    A_["xT"] = tiles(np.concatenate([x["x_prompt"][0], x["x_sample"][:, 0]], 0).T)
    A_["memT"] = tiles(x["mem_prompt"][0].T)
    A_["gvec"] = np.concatenate([columns(x[n][l]) for n in ("g_pre", "g_post", "g_mem") for l in range(2)], 1)
    A_["bf"] = x["fox_b_f"][0][:, None]
    w = x["fox_w_in"][0]
    tw = FH * P
    A_["wq"] = units(w[:, :tw])
    A_["wkv"] = np.stack([units(w[:, tw:2 * tw]), units(w[:, 2 * tw:3 * tw])], 1).reshape(12, P, KT * U)
    A_["wf"] = tiles(w[:, 3 * tw:3 * tw + FH])
    at = 3 * tw + FH
    A_["wqm0"] = units(w[:, at:at + MH * P])
    A_["wg0"] = units(w[:, at + MH * P:])
    for l in range(2):
        A_[f"wo{l}"] = units(x["w_o"][l])
        A_[f"wm{l}"] = units(x["w_mem"][l])
    w = x["rwkv_w_in"][0]
    at = 3 * tw + 2 * LORA
    A_["wl"] = units(w[:, 3 * tw:at], LORA)
    A_["wqm1"] = units(w[:, at:at + MH * P])
    A_["wg1"] = units(w[:, at + MH * P:])
    mu, sh = x["rwkv_mu"][0], x["state_rwkv_shift"][0][:, 0]
    rkv = w[:, :3 * tw].reshape(KT, P, 3, RP, P).transpose(3, 1, 0, 2, 4).reshape(RP, P, KT * RW)

    def lora(a):
        a = a.reshape(LORA, RP, P).transpose(1, 0, 2)
        return np.concatenate([a, np.zeros((RP, P - LORA, P), np.float32)], 1)

    vecs = [mu[:tw], mu[tw:2 * tw], mu[2 * tw:3 * tw]] + [x[n][0] for n in (
        "rwkv_w0", "rwkv_a0", "rwkv_k_k", "rwkv_k_a", "rwkv_r_k")]
    vecs = np.stack(vecs, 1).reshape(RP, P, 8)
    A_["lnv"] = np.stack([x[n][0] for n in ("rwkv_ln_w", "rwkv_ln_b")], 1).reshape(RP, P, 2).transpose(1, 0, 2).reshape(P, RP * 2)
    shift = sh[:, :3 * tw].reshape(NS, 3, RP, P).transpose(2, 3, 1, 0).reshape(RP, P, 3 * NS)
    A_["wrkv"] = rkv
    A_["vrkv"] = np.concatenate([lora(x["rwkv_w_w2"][0]), lora(x["rwkv_w_a2"][0]), vecs, shift], 2)

    def padded(a):
        return np.concatenate([a, np.zeros((P - LORA,) + a.shape[1:], np.float32)], 0)

    A_["muL"] = padded(mu[3 * tw:].reshape(2, LORA).T)
    A_["shL"] = padded(sh[:, 3 * tw:].reshape(NS, 2, LORA).transpose(2, 1, 0))
    A_["s0"] = x["state_rwkv_wkv"][0].reshape(NS, RP, 2, 64, 64).transpose(1, 2, 4, 0, 3).reshape(RP, P, NS * 64)
    A_["ck"] = x["cache_fox_k"][0].reshape(-1, P, PAGE_W)
    A_["cv"] = x["cache_fox_v"][0].reshape(-1, P, PAGE_W)
    A_["cf"] = x["cache_fox_logf"][0]
    A_["cmk"] = x["cache_mem_k"].reshape(2 * NS, NMEM, MH * P)
    A_["cmv"] = x["cache_mem_v"].reshape(2 * NS, NMEM, MH * P)
    A_["pt"] = x["page_table"].reshape(-1)

    nc = bacc.Bacc("TRN2", target_bir_lowering=False, num_devices=1)
    arrays, I, O = {}, {}, {}
    for n, a in A_.items():
        a = np.ascontiguousarray(a)
        arrays["in_" + n] = a
        I[n] = nc.dram_tensor("in_" + n, a.shape, mybir.dt.from_np(a.dtype), kind="ExternalInput").ap()
    for n, shape in _OUTS.items():
        O[n] = nc.dram_tensor("out_" + n, shape, F32, kind="ExternalOutput").ap()
    trunk_step(nc, I, O)
    res = run(nc, [arrays], core_ids=[0]).results[0]
    o = {n: res["out_" + n] for n in _OUTS}

    y = o["yT"].reshape(P, KT, T).transpose(2, 1, 0).reshape(T, D)
    mem = [o[n].reshape(2, P, MH, NMEM).transpose(0, 3, 2, 1)[:, None] for n in ("mk", "mv")]
    fox = [o[n].reshape(P, FH, T).transpose(2, 1, 0) for n in ("fk", "fv")]
    lf = o["lf"].T
    sh = o["sh"].reshape(P, SHT, 9).transpose(2, 1, 0)
    main = sh[:, :3 * RP].reshape(9, RP, 3, P).transpose(0, 2, 1, 3).reshape(9, 3 * tw)
    sh = np.concatenate([main, sh[:, 3 * RP, :LORA], sh[:, 3 * RP + 1, :LORA]], 1)
    wp = o["wp"].reshape(RP, 2, 64, 2, 64)
    wp = np.stack([wp[:, h, :, h, :] for h in range(2)], 1).transpose(0, 1, 3, 2).reshape(1, 1, 2 * RP, 64, 64)
    ws = o["ws"].reshape(RP, 2, 64, NS, 64).transpose(3, 0, 1, 4, 2).reshape(1, NS, 2 * RP, 64, 64)
    out = (y[None, :NPR], y[NPR:, None], mem[0], mem[1],
           fox[0][None, None, :NPR], fox[1][None, None, :NPR], lf[None, None, :NPR],
           fox[0][None, NPR:, None], fox[1][None, NPR:, None], lf[None, NPR:, None],
           wp, sh[None, None, 0:1], ws, sh[None, 1:, None])
    return tuple(np.ascontiguousarray(a) for a in out)
```
